# Optimizing a Trainium2 kernel written in Bass

```python
import jax, jax.numpy as jnp
from jax import lax
import numpy as np

D_MODEL = 1024
BATCH = 1
SEQ = 512
DEPTH = 1

SB_HEADS = 8
SB_HEAD_DIM = 64
SB_WIDTH = SB_HEADS * SB_HEAD_DIM
CONV_CHANNELS = 512
CONV_WIDTH = 3
MEM_TOKENS = 256
MEM_HEADS = 4
MEM_HEAD_DIM = 128
MEM_WIDTH = MEM_HEADS * MEM_HEAD_DIM
N_BRANCHES = 3
N_EXPERTS = 32
TOP_K = 4
D_FF_EXPERT = 1024
SWIGLU_LIMIT = 7.0
SWIGLU_ALPHA = 1.702
Q_BLOCK = 128
MOE_BLOCK = 128
RMS_EPS = 1e-6

IN_PARTS = (SB_WIDTH, SB_WIDTH, SB_WIDTH,
            CONV_CHANNELS, CONV_CHANNELS, CONV_CHANNELS,
            MEM_WIDTH, N_BRANCHES * D_MODEL)
IN_WIDTH = sum(IN_PARTS)
IN_SPLITS = tuple(int(v) for v in np.cumsum(IN_PARTS)[:-1])

kernel_name = "hybrid_stickbreak_shortconv_memattn_moe"

def rms_norm(x, g):
    xf = x.astype(jnp.float32)
    y = xf * lax.rsqrt(jnp.mean(xf * xf, axis=-1, keepdims=True) + RMS_EPS)
    return (y * g.astype(jnp.float32)).astype(x.dtype)

def stick_breaking_attention(q, k, v):
    b, s, h, dh = q.shape
    nb = s // Q_BLOCK
    scale = dh ** -0.5
    kt = k.transpose(0, 2, 1, 3).astype(jnp.float32)
    vt = v.transpose(0, 2, 1, 3).astype(jnp.float32)
    qb = q.reshape(b, nb, Q_BLOCK, h, dh).transpose(1, 0, 3, 2, 4)
    key_pos = jnp.arange(s)

    def block(args):
        q_blk, blk = args
        z = jnp.einsum('bhqd,bhkd->bhqk', q_blk.astype(jnp.float32), kt) * scale
        q_pos = blk * Q_BLOCK + jnp.arange(Q_BLOCK)
        causal = key_pos[None, :] < q_pos[:, None]
        log_stay = jnp.where(causal, jax.nn.log_sigmoid(-z), 0.0)
        log_between = lax.cumsum(log_stay, axis=3, reverse=True) - log_stay
        w = jnp.where(causal, jnp.exp(jax.nn.log_sigmoid(z) + log_between), 0.0)
        return jnp.einsum('bhqk,bhkd->bhqd', w, vt)

    o = lax.map(block, (qb, jnp.arange(nb)))
    return o.transpose(1, 0, 3, 2, 4).reshape(b, s, h * dh).astype(q.dtype)

def short_gated_conv(u_b, u_c, u_x, conv_w):
    c = u_x.shape[-1]
    u = u_c * u_x
    z = lax.conv_general_dilated(
        u, conv_w[:, None, :].astype(u.dtype), window_strides=(1,),
        padding=[(CONV_WIDTH - 1, 0)], dimension_numbers=('NWC', 'WIO', 'NWC'),
        feature_group_count=c)
    return u_b * z

def memory_attention(q, mem_n, w_mem_kv, q_g, k_g):
    b, s, _ = q.shape
    m = mem_n.shape[1]
    kv = mem_n @ w_mem_kv
    k, v = jnp.split(kv, 2, axis=-1)
    q = rms_norm(q.reshape(b, s, MEM_HEADS, MEM_HEAD_DIM), q_g)
    k = rms_norm(k.reshape(b, m, MEM_HEADS, MEM_HEAD_DIM), k_g)
    v = v.reshape(b, m, MEM_HEADS, MEM_HEAD_DIM)
    sc = jnp.einsum('bshd,bmhd->bhsm', q.astype(jnp.float32), k.astype(jnp.float32)) * (MEM_HEAD_DIM ** -0.5)
    p = jax.nn.softmax(sc, axis=-1)
    o = jnp.einsum('bhsm,bmhd->bshd', p, v.astype(jnp.float32))
    return o.reshape(b, s, MEM_WIDTH).astype(q.dtype)

def moe_ffn(h, w_router, b_router, w_gate_up, b_gate_up, w_down, b_down):
    t, d = h.shape
    a = t * TOP_K
    logits = (h @ w_router + b_router).astype(jnp.float32)
    top_val, top_idx = lax.top_k(logits, TOP_K)
    gate = jax.nn.softmax(top_val, axis=-1)
    flat_e = top_idx.reshape(a)
    flat_tok = jnp.arange(a) // TOP_K
    order = jnp.argsort(flat_e, stable=True)
    e_sorted = flat_e[order]
    counts = jnp.bincount(flat_e, length=N_EXPERTS)
    padded = (counts + MOE_BLOCK - 1) // MOE_BLOCK * MOE_BLOCK
    start = jnp.cumsum(counts) - counts
    pend = jnp.cumsum(padded)
    pstart = pend - padded
    dest = pstart[e_sorted] + (jnp.arange(a) - start[e_sorted])
    n_blocks = -(-a // MOE_BLOCK) + N_EXPERTS
    n_rows = n_blocks * MOE_BLOCK
    x_pad = jnp.zeros((n_rows, d), h.dtype).at[dest].set(h[flat_tok[order]])
    block_e = jnp.clip(jnp.searchsorted(pend, jnp.arange(n_blocks) * MOE_BLOCK, side='right'), 0, N_EXPERTS - 1)

    def expert_block(args):
        xb, e = args
        gu = xb @ w_gate_up[e] + b_gate_up[e]
        g, lin = jnp.split(gu, 2, axis=-1)
        g = jnp.minimum(g, SWIGLU_LIMIT)
        lin = jnp.clip(lin, -SWIGLU_LIMIT, SWIGLU_LIMIT)
        act = g * jax.nn.sigmoid(SWIGLU_ALPHA * g) * (lin + 1.0)
        return act @ w_down[e] + b_down[e]

    y_pad = lax.map(expert_block, (x_pad.reshape(n_blocks, MOE_BLOCK, d), block_e)).reshape(n_rows, d)
    y_assign = jnp.zeros((a, d), y_pad.dtype).at[order].set(y_pad[dest]).reshape(t, TOP_K, d)
    return jnp.einsum('tk,tkd->td', gate.astype(y_assign.dtype), y_assign)

def setup_inputs(seed: int = 0) -> dict:
    key = jax.random.key(seed)
    ks = jax.random.split(key, 24)
    f32 = jnp.float32
    nrm = lambda k, shape, s: jax.random.normal(k, shape, f32) * s
    gain = lambda k, shape: 1.0 + 0.02 * jax.random.normal(k, shape, f32)
    L, D, E, F = DEPTH, D_MODEL, N_EXPERTS, D_FF_EXPERT
    return {
        "x": nrm(ks[0], (BATCH, SEQ, D), 1.0),
        "mem": nrm(ks[1], (BATCH, MEM_TOKENS, D), 1.0),
        "mix_norm_g": gain(ks[2], (L, D)),
        "w_in": nrm(ks[3], (L, D, IN_WIDTH), D ** -0.5),
        "sb_q_norm_g": gain(ks[4], (L, SB_HEAD_DIM)),
        "sb_k_norm_g": gain(ks[5], (L, SB_HEAD_DIM)),
        "conv_w": nrm(ks[6], (L, CONV_WIDTH, CONV_CHANNELS), CONV_WIDTH ** -0.5),
        "mem_norm_g": gain(ks[7], (L, D)),
        "w_mem_kv": nrm(ks[8], (L, D, 2 * MEM_WIDTH), D ** -0.5),
        "mem_q_norm_g": gain(ks[9], (L, MEM_HEAD_DIM)),
        "mem_k_norm_g": gain(ks[10], (L, MEM_HEAD_DIM)),
        "w_br_sb": nrm(ks[11], (L, SB_WIDTH, D), SB_WIDTH ** -0.5),
        "w_br_conv": nrm(ks[12], (L, CONV_CHANNELS, D), CONV_CHANNELS ** -0.5),
        "w_br_mem": nrm(ks[13], (L, MEM_WIDTH, D), MEM_WIDTH ** -0.5),
        "w_o": nrm(ks[14], (L, D, D), D ** -0.5),
        "ffn_norm_g": gain(ks[15], (L, D)),
        "w_router": nrm(ks[16], (L, D, E), D ** -0.5),
        "b_router": nrm(ks[17], (L, E), 0.01),
        "w_gate_up": nrm(ks[18], (L, E, D, 2 * F), D ** -0.5),
        "b_gate_up": nrm(ks[19], (L, E, 2 * F), 0.01),
        "w_down": nrm(ks[20], (L, E, F, D), F ** -0.5),
        "b_down": nrm(ks[21], (L, E, D), 0.01),
    }

def reference(x, mem, mix_norm_g, w_in, sb_q_norm_g, sb_k_norm_g, conv_w, mem_norm_g,
              w_mem_kv, mem_q_norm_g, mem_k_norm_g, w_br_sb, w_br_conv, w_br_mem, w_o,
              ffn_norm_g, w_router, b_router, w_gate_up, b_gate_up, w_down, b_down):
    b, s, d = x.shape
    for l in range(DEPTH):
        h = rms_norm(x, mix_norm_g[l])
        proj = h @ w_in[l]
        q_sb, k_sb, v_sb, cb, cc, cx, q_mem, gates = jnp.split(proj, IN_SPLITS, axis=-1)
        q_sb = rms_norm(q_sb.reshape(b, s, SB_HEADS, SB_HEAD_DIM), sb_q_norm_g[l])
        k_sb = rms_norm(k_sb.reshape(b, s, SB_HEADS, SB_HEAD_DIM), sb_k_norm_g[l])
        v_sb = v_sb.reshape(b, s, SB_HEADS, SB_HEAD_DIM)
        o_sb = stick_breaking_attention(q_sb, k_sb, v_sb)
        o_conv = short_gated_conv(cb, cc, cx, conv_w[l])
        mem_n = rms_norm(mem, mem_norm_g[l])
        o_mem = memory_attention(q_mem, mem_n, w_mem_kv[l], mem_q_norm_g[l], mem_k_norm_g[l])
        g = jax.nn.sigmoid(gates.reshape(b, s, N_BRANCHES, d))
        merged = (g[:, :, 0] * (o_sb @ w_br_sb[l])
                  + g[:, :, 1] * (o_conv @ w_br_conv[l])
                  + g[:, :, 2] * (o_mem @ w_br_mem[l]))
        x = x + merged @ w_o[l]
        hf = rms_norm(x, ffn_norm_g[l]).reshape(b * s, d)
        y = moe_ffn(hf, w_router[l], b_router[l], w_gate_up[l], b_gate_up[l], w_down[l], b_down[l])
        x = x + y.reshape(b, s, d).astype(x.dtype)
    return x


_drawn_inputs = setup_inputs


def setup_inputs(seed=0):
    import zlib

    import numpy as np

    out = dict(_drawn_inputs(seed))
    spreads = {}
    factors = {'sb_q_norm_g': 27.816,
     'sb_k_norm_g': 39.432,
     'mem_norm_g': 8.0,
     'mem_q_norm_g': 8.0,
     'mem_k_norm_g': 8.0,
     'b_gate_up': 40.214,
     'b_down': 46.147,
     'ffn_norm_g': 5.285,
     'b_router': 7.569}
    for name, (base, spread) in spreads.items():
        noise = np.random.default_rng([zlib.crc32(name.encode()), seed]).standard_normal(out[name].shape)
        drawn = base * np.exp(spread * noise) if base else spread * noise
        out[name] = __import__('jax').numpy.asarray(drawn.astype(out[name].dtype))
    for name, factor in factors.items():
        out[name] = (out[name] * factor).astype(out[name].dtype)
    return out
```

```python
from contextlib import ExitStack

import concourse.bass as bass
from concourse import mybir

F32 = mybir.dt.float32
F32R = mybir.dt.float32r
BF16 = mybir.dt.bfloat16
U32 = mybir.dt.uint32
ALU = mybir.AluOpType
ACT = mybir.ActivationFunctionType
AX = mybir.AxisListType

P = 128
SEQ, D = 512, 1024
NT = SEQ // P
KD = D // P
MEM, MT = 256, 2
SBH, DH = 8, 64
MH = 4
G = 512
E, FF, TOPK = 32, 1024, 4
LIMIT, ALPHA, EPS = 7.0, 1.702, 1e-6
BLK = 128
NBLK = SEQ // BLK
COLS = NBLK * E
NEVER = 1 << 20
MASKED = -1e30

SLOTS = 6
BUFS = 4
SLOTS_MIX = 4
GU, DN = 8, 4

GROUPS = {"mk": (2, MEM, 4), "q": (2, SEQ, 4), "k": (2, SEQ, 4), "qm": (2, SEQ, 4), "mv": (2, G, MT), "v": (2, G, NT),
          "cc": (2, SEQ, 4), "cx": (2, SEQ, 4), "cb": (2, SEQ, 4)}
for _i in range(3):
    for _j in range(2):
        GROUPS[f"g{_i}{_j}"] = (2, SEQ, 4)
        GROUPS[f"b{_i}{_j}"] = (1, SEQ, 4)
for _j in range(2):
    GROUPS[f"o{_j}"] = (2, G, NT)
NORMED = ("mk", "q", "k", "qm")
TOKEN_MAJOR = ("mv", "v", "o0", "o1")
EARLY_GATES = ("g00", "g01", "g10")
W_IN_COLUMN = {"q": 0, "k": 1, "v": 2, "cb": 3, "cc": 4, "cx": 5, "qm": 6, "g00": 7, "g01": 8, "g10": 9, "g11": 10,
               "g20": 11, "g21": 12}


def plan_mixer():
    tiles, steps = [], []
    order = ["mk", "q", "k", "qm", "mv", "v", "cc", "cx", "cb", *EARLY_GATES, "b00", "b01", "b10", "g11", "b11",
             "g20", "b20", "g21", "b21", "o0", "o1"]
    for g in order:
        for t in range(GROUPS[g][0]):
            tiles.append((g, t))
    number = {x: n for n, x in enumerate(tiles)}

    def units(g):
        for t in range(GROUPS[g][0]):
            for c in range(GROUPS[g][2]):
                out = []
                if c == 0 and number[g, t] + 1 < len(tiles):
                    out.append(("split", number[g, t] + 1))
                out.append(("unit", g, t, c))
                if t == GROUPS[g][0] - 1:
                    out.append(("save", g, c))
                yield out

    steps.append(("split", 0))
    late = []
    for g in ("mk", "q", "k", "qm", "mv", "v"):
        for part in units(g):
            steps += part
            for x in late:
                steps.append(("ssum", *x))
                steps.append(("norm", *x))
            late = [part[-1][1:]] if part[-1][0] == "save" and g in NORMED else []
    beside = [part for g in ("cc", "cx", "cb") for part in units(g)]
    for h in range(MH):
        steps += [("mscore", h), ("msoft", h)]
        for _ in range(4):
            steps += beside.pop(0)
        steps += [("mturn", h)]
        for _ in range(2):
            steps += beside.pop(0)
        steps += [("mout", h)]
    beside = [part for g in EARLY_GATES for part in units(g)]
    for h in range(SBH):
        steps += [("z", h), ("soft", h)]
        for _ in range(2):
            steps += beside.pop(0)
        steps += [("between", h)]
        steps += beside.pop(0)
        steps += [("av", h)]
    assert not beside
    steps += [("osplit", 0), ("sig", 0), ("osplit", 1), ("sig", 1), ("osplit", 2), ("sig", 2)]
    for g in order[order.index("b00"):]:
        for part in units(g):
            steps += part
    return tiles, number, steps


TILES, NUMBER, STEPS = plan_mixer()
NM = len(TILES)


def ranks(keys):
    return {k: n + 1 for n, k in enumerate(keys)}


SAVES = [s[1:] for s in STEPS if s[0] == "save"]
BY_ACT = lambda g: g in (*NORMED, "mv", "v", "cc") or g[0] == "g"
SAVED_ACT = ranks(x for x in SAVES if BY_ACT(x[0]))
SAVED_DVE = ranks(x for x in SAVES if not BY_ACT(x[0]))
DONE_UNIT = ranks(SAVES)
NORMS = ranks(s[1:] for s in STEPS if s[0] == "norm")
BANK, FREED_BY = {}, {}
_last, _side = {}, 0
for _g in dict.fromkeys(x[0] for x in SAVES):
    _merge = _g[0] in "bo" or (_g[0] == "g" and _g not in EARLY_GATES)
    _side = 4 - _side if _merge else 0
    for _c in range(GROUPS[_g][2]):
        BANK[_g, _c] = _side + _c
        FREED_BY[_g, _c] = _last.get(_side + _c)
        _last[_side + _c] = (_g, _c)

WIDTH = [SEQ - P * i for i in range(NT)]
OFF = [sum(WIDTH[:i]) for i in range(NT)]
PACKED = sum(WIDTH)


def build(nc, a, out, stop_after_mixer=False):
    with ExitStack() as ctx:
        ctx.enter_context(nc.allow_non_contiguous_dma("small vectors laid along the partitions"))
        base = 16512

        def sb(name, shape, dt, kb):
            return nc.alloc_sbuf_tensor_at(name, shape, dt, offset=base + int(kb * 1024))

        def sem(name):
            return ctx.enter_context(nc.semaphore(name))

        ps = ctx.enter_context(nc.psum_tensor("ps", [P, 8, 512], F32))

        ring = sb("ring", [P, SLOTS, 2048], F32, 0)
        hh = sb("hh", [P, KD, SEQ], F32R, 32)
        hl = sb("hl", [P, KD, SEQ], F32R, 48)
        qT = sb("qT", [P, 4, SEQ], F32, 64)
        kT = sb("kT", [P, 4, SEQ], F32, 72)
        v = sb("v", [P, NT, G], F32, 80)
        cu = sb("cu", [P, 4, SEQ], F32, 88)
        we = sb("we", [P, PACKED], F32, 88)
        oh = [sb("o0h", [P, 4, SEQ], F32R, 64), sb("o1h", [P, 4, SEQ], F32R, 80), sb("o2h", [P, 4, SEQ], F32R, 186)]
        ol = [sb("o0l", [P, 4, SEQ], F32R, 72), sb("o1l", [P, 4, SEQ], F32R, 88), sb("o2l", [P, 4, SEQ], F32R, 194)]
        gh = sb("gh", [P, KD, SEQ], F32R, 64)
        gl = sb("gl", [P, KD, SEQ], F32R, 80)
        xr = sb("xr", [P, NT, D], F32, 32)
        x2 = sb("x2", [P, NT, D], F32, 48)
        wh = sb("wh", [P, 2, 2048], F32R, 96)
        wl = sb("wl", [P, 2, 2048], F32R, 112)
        ident = sb("ident", [P, P], F32, 128)
        ones = sb("ones", [P, P], F32, 128.5)
        halves = sb("halves", [P, P], F32, 129)
        down = sb("down", [P, P], F32R, 129.5)
        minus = sb("minus", [P, P], F32R, 130)
        identb = sb("identb", [P, P], BF16, 130.5)
        maskb = sb("maskb", [P, P], BF16, 130.75)
        before = sb("before", [P, P], BF16, 131)
        onesb = sb("onesb", [P, P], BF16, 131.25)
        downf = sb("downf", [P, P], F32, 131.5)
        gbc = sb("gbc", [P, D], F32, 132)
        small = sb("small", [P, 384], F32, 136)
        xm = sb("xm", [P, NT + MT, D], F32, 138)
        mh = sb("mh", [P, KD, MEM], F32R, 162)
        ml = sb("ml", [P, KD, MEM], F32R, 170)
        sqd = sb("sqd", [P, D], F32, 186)
        km = sb("km", [P, MH, MEM], F32, 138)
        vm = sb("vm", [P, MT, G], F32, 142)
        osb = sb("osb", [P, 4, SEQ], F32, 138)
        om = sb("om", [P, 4, SEQ], F32, 146)
        oc = sb("oc", [P, 4, SEQ], F32, 154)
        qm = sb("qm", [P, MH, SEQ], F32, 178)
        gate = sb("gate", [P, 3, 4, SEQ], F32, 162)
        nsq = sb("nsq", [P, 2, SEQ], F32, 186)
        nm_ = sb("nm_", [P, 2, SEQ], F32, 190)
        ny = sb("ny", [P, 2, SEQ], F32, 194)
        nt_ = sb("nt_", [P, 2, SEQ], F32, 198)
        pm = sb("pm", [P, NT, MEM], F32, 186)
        pT = sb("pT", [P, MT, SEQ], F32, 190)
        sp = sb("sp", [P, PACKED], F32, 186)
        sph = sb("sph", [P, PACKED], F32R, 191)
        spl = sb("spl", [P, PACKED], F32R, 196)
        w = sb("w", [P, PACKED], F32, 201)

        acc = sb("acc", [P, KD, SEQ], F32, 138)
        tmp = sb("tmp", [P, 2, SEQ], F32, 202)
        sq2 = sb("sq2", [P, D], F32, 138)
        hf = sb("hf", [P, NT, D], F32, 154)
        hfT = sb("hfT", [P, KD, SEQ], F32, 170)
        rt = sb("rt", [P, 1740], F32, 186)
        eh = sb("eh", [P, BUFS, 2048], F32R, 64)
        el = sb("el", [P, BUFS, 2048], F32R, 96)
        ebias = sb("ebias", [3 * E, 3 * FF], BF16, 198)
        braw = sb("braw", [3 * E, 3 * FF], F32, 84)
        pick = sb("pick", [3 * E, E * P], BF16, 146)
        xg = sb("xg", [P, D], F32, 154)
        xh = sb("xh", [P, KD, P], F32R, 158)
        xl = sb("xl", [P, KD, P], F32R, 162)
        gm = sb("gm", [P, FF], F32, 166)
        lc = sb("lc", [P, FF], F32, 170)
        sg = sb("sg", [P, FF], F32, 174)
        ac = sb("ac", [P, FF], F32, 178)
        ah = sb("ah", [P, KD, P], F32R, 182)
        al = sb("al", [P, KD, P], F32R, 186)
        yo = sb("yo", [P, D], F32, 190)
        tok = sb("tok", [P, COLS], U32, 204)
        row = sb("row", [P, COLS], U32, 205)
        gw = sb("gw", [P, NT, TOPK], F32, 206.25)
        now = sb("now", [P, 4], U32, 206.5)
        most = sb("most", [P, 4], U32, 206.625)
        wide = sb("wide", [P, GU, 2048], F32, 64)
        xf = sb("xf", [P, KD, P], F32, 158)
        af = sb("af", [P, KD, P], F32, 182)
        yg = sb("yg", [P, NT, TOPK, D], F32, 64)

        def cols(a0, n):
            return small[:, a0:a0 + n]
        mixg, memg = cols(0, KD), cols(8, KD)
        qg, kg, qmg, kmg = cols(16, 1), cols(17, 1), cols(18, 1), cols(19, 1)
        taps = cols(20, 12)
        ssx, mx_, rx, tx = cols(32, 6), cols(38, 6), cols(44, 6), cols(50, 6)
        mmax, mneg_, msum, mrec = cols(56, 4), cols(60, 4), cols(64, 4), cols(68, 4)
        ss2, m2, r2, t2 = cols(72, 4), cols(76, 4), cols(80, 4), cols(84, 4)
        gneg, gsum, grec = cols(88, 4), cols(92, 4), cols(120, 4)
        bro = small[0:1, 328:360]
        wr = sb("wr", [P, KD, E], F32, 194)

        def rcols(a0, n, m=None):
            x = rt[:, a0:a0 + n]
            return x if m is None else x.rearrange("p (a b) -> p a b", b=m)
        lg = rcols(0, 128, E)
        v8 = rcols(128, 32, 8)
        i8f = rcols(160, 32, 8)
        oneh = rcols(192, 512, E)
        msk = rcols(704, 128, E)
        posf = rcols(832, 128, E)
        junk = rcols(960, 128)
        pk, jj, tif = rcols(1088, 16), rcols(1120, 16), rcols(1136, 16)
        iotaf = rcols(1152, 32)
        i8 = sb("i8", [P, NT, 8], U32, 193)
        ti = sb("ti", [P, NT * TOPK], U32, 193.25)
        rows = sb("rows", [P, NT * TOPK], U32, 193.375)
        never = sb("never", [P, COLS], U32, 195)
        mskb = sb("mskb", [P, NT, E], BF16, 193.5)
        iotai = sb("iotai", [P, E], U32, 193.75)

        hf_d = nc.dram_tensor("hf_scratch", (SEQ, D), F32).ap()
        slot_d = nc.dram_tensor("slot_scratch", (P * COLS, 1), U32).ap()
        y_d = nc.dram_tensor("y_scratch", (SEQ * TOPK, D), F32).ap()

        small_in = sem("small_in")
        xm_in = [sem(f"xm_in{r}") for r in range(NT + MT)]
        w_in = [sem(f"w_in{s}") for s in range(SLOTS)]
        made = sem("made")
        made_dve = sem("made_dve")
        squared = sem("squared")
        mean_ready, root_ready, scaled = sem("mean_ready"), sem("root_ready"), sem("scaled")
        turned, h_hi, h_lo = sem("turned"), sem("h_hi"), sem("h_lo")
        w_hi, w_lo = sem("w_hi"), sem("w_lo")
        unit_done, saved_act, saved_dve = sem("unit_done"), sem("saved_act"), sem("saved_dve")
        nsq_ready, ssum_done, nm_ready, ny_ready, normed = (sem(x) for x in ("nsq_ready", "ssum_done", "nm_ready", "ny_ready", "normed"))
        ms_done, mneg_ready, mexp_done, mprob_ready, mt_done, mt_act, mt_dve, mo_done, om_saved = (
            sem(x) for x in ("ms_done", "mneg_ready", "mexp_done", "mprob_ready", "mt_done", "mt_act", "mt_dve", "mo_done", "om_saved"))
        z_done, log_done, sp_done, sph_done, spl_done, c_done, w_done, av_done, o_saved = (
            sem(x) for x in ("z_done", "log_done", "sp_done", "sph_done", "spl_done", "c_done", "w_done", "av_done", "o_saved"))
        oh_done, osplit_done, sig_done, acc_done, gh_done, gl_done = (
            sem(x) for x in ("oh_done", "osplit_done", "sig_done", "acc_done", "gh_done", "gl_done"))
        xr_in, squared2, m2_ready, r2_ready, hf_done, hf_turned, hfT_act, hfT_dve, logit_done = (
            sem(x) for x in ("xr_in", "squared2", "m2_ready", "r2_ready", "hf_done", "hf_turned", "hfT_act", "hfT_dve", "logit_done"))
        x2_out, hf_out = sem("x2_out"), sem("hf_out")
        act_step, dve_step, pool_step = sem("act_step"), sem("dve_step"), sem("pool_step")
        out_done = sem("out_done")

        def operands(g):
            if g[0] == "m":
                return mh, ml
            if g[0] == "b":
                return oh[int(g[1])], ol[int(g[1])]
            return (gh, gl) if g[0] == "o" else (hh, hl)

        def weight_source(g, t):
            lo, hi = t * 4 * P, (t + 1) * 4 * P
            if g in W_IN_COLUMN:
                src, c = a["w_in"][0], W_IN_COLUMN[g] * G
            elif g in ("mk", "mv"):
                src, c = a["w_mem_kv"][0], G * (g == "mv")
            elif g[0] == "b":
                src, c = a[("w_br_sb", "w_br_conv", "w_br_mem")[int(g[1])]][0], int(g[2]) * G
            else:
                src, c = a["w_o"][0], int(g[1]) * G
            return src[lo:hi, c:c + G].rearrange("(k p) n -> p k n", p=P)

        UNIT = ranks(s[1:] for s in STEPS if s[0] == "unit")
        USED = {n: UNIT[g, t, GROUPS[g][2] - 1] for n, (g, t) in enumerate(TILES)}
        SUMMED = {(g, c): UNIT[g, GROUPS[g][0] - 1, c] for g, c in SAVES}
        LATE = {"g11": (0, "b00"), "g20": (1, "b01"), "g21": (2, "b10")}
        PLACE = {"b00": 0, "b01": 1, "b10": 2, "b11": 0, "b20": 1, "b21": 2}
        T0 = NT
        TURNS = [("m", k) for k in range(KD)] + [("x", k) for k in range(KD)]

        def split(n):
            return wh[:, n % 2, :], wl[:, n % 2, :]

        def chunk(g, c, half=None):
            n = GROUPS[g][1]
            return ps[:, BANK[g, c], 0:n]

        def normed_chunk(g, c):
            return {"mk": km, "q": qT, "k": kT, "qm": qm}[g][:, c, :]

        GAIN = {"mk": kmg, "q": qg, "k": kg, "qm": qmg}
        SCALE_M = float(P) ** -0.5

        MADE = 15
        small_loads = [(mixg, a["mix_norm_g"][0].rearrange("(k p) -> p k", p=P)), (memg, a["mem_norm_g"][0].rearrange("(k p) -> p k", p=P)),
                       (qmg, a["mem_q_norm_g"][0].rearrange("(p o) -> p o", o=1)), (kmg, a["mem_k_norm_g"][0].rearrange("(p o) -> p o", o=1)),
                       (bro, a["b_router"]), (gbc[:, :], a["ffn_norm_g"].broadcast_to([P, D]))]
        for half in range(2):
            for dst, name in ((qg, "sb_q_norm_g"), (kg, "sb_k_norm_g")):
                small_loads.append((dst[half * DH:(half + 1) * DH, :], a[name][0].rearrange("(p o) -> p o", o=1)))
        for j in range(3):
            small_loads.append((taps[:, 4 * j:4 * j + 4], a["conv_w"][0][j].rearrange("(c p) -> p c", p=P)))


        slot_set, slot_in, slot_out, tok_ready, most_ready = (
            sem(x) for x in ("slot_set", "slot_in", "slot_out", "tok_ready", "most_ready"))
        wr_in, rmade, best_ready, gexp_done, msk_ready, pos_done, ti_ready, braw_in, ebias_ready, picks_ready = (
            sem(x) for x in ("wr_in", "rmade", "best_ready", "gexp_done", "msk_ready", "pos_done", "ti_ready", "braw_in", "ebias_ready", "picks_ready"))
        e_used = sem("e_used")
        xg_in, x_turned, xh_done, x_split = (sem(x) for x in ("xg_in", "x_turned", "xh_done", "x_split"))
        lin_done, pool_now = sem("lin_done"), sem("pool_now")
        gu_free, gm_done, sg_done, ac_done, a_turned, ah_done, a_split = (
            sem(x) for x in ("gu_free", "gm_done", "sg_done", "ac_done", "a_turned", "ah_done", "a_split"))
        dn_free, y_out = sem("dn_free"), sem("y_out")
        more_x, more_xf, more_gu, more_act, more_lin, more_af, more_dn, more_y, more_sig, more_w, more_turn = (
            sem(x) for x in ("more_x", "more_xf", "more_gu", "more_act", "more_lin", "more_af", "more_dn", "more_y", "more_sig",
                             "more_w", "more_turn"))
        xb_in = sem("xb_in")
        yg_in = [sem(f"yg_in{t}") for t in range(NT)]
        summed = sem("summed")

        SIDE = BANK["o0", 0]
        LOGIT = BANK["o1", 0]
        ROUTE = SIDE
        USES = NM // SLOTS_MIX
        assert NM % SLOTS_MIX == 0 and NM % 2 == 0
        PER = GU + DN

        def at(e, n):
            return NM + n if isinstance(e, int) and e == 0 else e * PER + (NM - DN + n)

        def gate_up(e, k):
            return a["w_gate_up"][0][e, k * P:(k + 1) * P, :]

        def down_tile(e, m):
            return a["w_down"][0][e, m * 2 * P:(m + 1) * 2 * P, :].rearrange("(k p) n -> p k n", p=P)

        def landed(eng, e, n):
            s, again = n % SLOTS, n // SLOTS
            before_it = USES if s < SLOTS_MIX else 0
            if isinstance(e, int) and e == 0:
                eng.wait_ge(w_in[s], 16 * (before_it + again + 1))
            else:
                first = 2 if s + SLOTS < GU else 1
                eng.wait_ge(w_in[s], e * (16 * PER // SLOTS) + 16 * (before_it + first - PER // SLOTS + again + 1))

        def iterations(eng, body):
            for e in range(3):
                body(e)
            with eng.Fori(3, E) as e:
                body(e)
            body(None)

        def experts_sync(sp_):
            def load(e, n):
                if isinstance(e, int) and e == 0:
                    if n >= SLOTS:
                        sp_.wait_ge(w_lo, at(0, n - SLOTS) + 1)
                    elif n < SLOTS_MIX:
                        sp_.wait_ge(w_lo, NM - SLOTS_MIX + n + 1)
                    else:
                        sp_.wait_ge(saved_dve, SAVED_DVE["o1", NT - 1])
                elif n >= SLOTS:
                    sp_.wait_ge(w_lo, at(e, n - SLOTS) + 1)
                elif isinstance(e, int) and e == 1:
                    sp_.wait_ge(w_lo, at(0, n + SLOTS if n + SLOTS < GU else n) + 1)
                else:
                    sp_.wait_ge(w_lo, at(e - 1, n + SLOTS) + 1)
                slot = ring[:, n % SLOTS, :]
                if n < GU:
                    sp_.dma_start(slot, gate_up(e, n)).then_inc(w_in[n % SLOTS], 16)
                else:
                    sp_.dma_start(slot.rearrange("p (k n) -> p k n", k=2), down_tile(e - 1, n - GU)).then_inc(w_in[n % SLOTS], 16)

            def body(e):
                if e is None:
                    for m in range(DN):
                        sp_.wait_ge(w_lo, at(E - 1, m + SLOTS) + 1)
                        sp_.dma_start(ring[:, m, :].rearrange("p (k n) -> p k n", k=2), down_tile(E - 1, m)).then_inc(w_in[m], 16)
                    return
                for n in range(GU if isinstance(e, int) and e == 0 else PER):
                    load(e, n)

            iterations(sp_, body)
            sp_.wait_ge(most_ready, 1)
            sp_.wait_ge(y_out, 16 * E)
            many = sp_.value_load(most[0:1, 0:1], min_val=0, max_val=SEQ)
            with sp_.If(many > BLK):
                with sp_.Fori(1, NBLK) as j:
                    with sp_.Fori(0, E) as e:
                        sp_.wait_ge(y_out, (j * E + e) * 16)
                        for k in range(GU):
                            sp_.dma_start(wide[:, k, :], gate_up(e, k)).then_inc(more_w, 16)
                        for m in range(DN):
                            sp_.dma_start(ring[:, m, :].rearrange("p (k n) -> p k n", k=2), down_tile(e, m)).then_inc(more_w, 16)
                sp_.wait_ge(y_out, 16 * E * NBLK)
            for t in range(NT):
                sp_.dma_start(yg[:, t, :, :], y_d.rearrange("(t p k) d -> t p k d", p=P, k=TOPK)[t]).then_inc(yg_in[t], 16)
            for t in range(NT):
                sp_.wait_ge(summed, 1 + t)
                sp_.dma_start(out[0][t * P:(t + 1) * P, :], x2[:, t, :]).then_inc(out_done, 16)
            sp_.wait_ge(out_done, 16 * NT)

        def routing_act(act, steps_seen):
            seen = [steps_seen]

            def step_(ins):
                seen[0] += 1
                ins.then_inc(act_step, 1)
                act.wait_ge(act_step, seen[0])

            act.wait_ge(gl_done, KD)
            for t in range(NT):
                act.wait_ge(saved_dve, SAVED_DVE["o1", t])
                if t:
                    act.wait_ge(squared2, t)
                act.activation(sq2[:, :], x2[:, t, :], ACT.Square, accum_out=ss2[:, t:t + 1]).then_inc(squared2, 1)
            act.wait_ge(m2_ready, 1)
            step_(act.activation(r2, m2, ACT.Ln))
            act.activation(r2, r2, ACT.Exp, scale=-0.5).then_inc(r2_ready, 1)
            for t in range(NT):
                act.wait_ge(hf_done, t + 1)
                act.dma_start(hf_d[t * P:(t + 1) * P, :], hf[:, t, :]).then_inc(hf_out, 16)
                act.wait_ge(hf_turned, t + 1)
                act.activation(hfT[:, 0:4, t * P:(t + 1) * P], ps[:, SIDE + 2 * (t % 2), :].rearrange("p (k n) -> p k n", k=4),
                               ACT.Copy).then_inc(hfT_act, 1)
            act.wait_ge(best_ready, 1)
            for t in range(NT):
                i_ = act.activation(gw[:, t, :], v8[:, t, 0:TOPK], ACT.Exp, bias=gneg[:, t:t + 1], accum_out=gsum[:, t:t + 1])
            i_.then_inc(gexp_done, 1)

            def hi_split(e, n):
                landed(act, e, n)
                if isinstance(e, int) and e == 0:
                    if n == 0:
                        act.wait_ge(unit_done, USED[NM - 1])
                    if n == 2:
                        act.wait_ge(ebias_ready, 1)
                    if n >= BUFS:
                        act.wait_ge(e_used, n - BUFS + 1)
                else:
                    act.wait_ge(e_used, e * PER + (n + 1 - DN - BUFS))
                act.activation(eh[:, n % BUFS, :], ring[:, n % SLOTS, :], ACT.Copy).then_inc(w_hi, 1)

            def x_hi(e):
                act.wait_ge(x_turned, e + 1)
                for z_ in range(2):
                    i_ = act.activation(xh[:, 4 * z_:4 * z_ + 4, :], ps[:, 6 + z_, :].rearrange("p (k n) -> p k n", k=4), ACT.Copy)
                i_.then_inc(xh_done, 1)

            def a_hi(e):
                act.wait_ge(a_turned, e + 1)
                for z_ in range(2):
                    i_ = act.activation(ah[:, 4 * z_:4 * z_ + 4, :], ps[:, 6 + z_, :].rearrange("p (k n) -> p k n", k=4), ACT.Copy)
                i_.then_inc(ah_done, 1)

            def sig(e):
                act.wait_ge(gm_done, e + 1)
                act.activation(sg[:, :], gm[:, :], ACT.Sigmoid, scale=ALPHA).then_inc(sg_done, 1)

            def save_y(e, used):
                act.wait_ge(e_used, used)
                if not (isinstance(e, int) and e == 0):
                    act.wait_ge(y_out, e * 16)
                for z_ in range(2):
                    i_ = act.activation(yo[:, 512 * z_:512 * z_ + 512], ps[:, 4 + z_, :], ACT.Copy)
                i_.then_inc(dn_free, 1)

            def body(e):
                if e is None:
                    for m in range(DN):
                        hi_split(E, m)
                        if m == 1:
                            save_y(E - 2, E * PER - DN)
                    a_hi(E - 1)
                    save_y(E - 1, E * PER)
                    return
                first = isinstance(e, int) and e == 0
                for n in range(GU if first else PER):
                    hi_split(e, n)
                    if n == 1 and not (isinstance(e, int) and e < 2):
                        save_y(e - 2, e * PER - DN)
                    if n == BUFS - 1 and not first:
                        a_hi(e - 1)
                x_hi(e + 1)
                sig(e)

            x_hi(0)
            iterations(act, body)
            act.wait_ge(y_out, 16 * E)
            act.wait_ge(most_ready, 1)
            many = act.value_load(most[0:1, 0:1], min_val=0, max_val=SEQ)
            with act.If(many > BLK):
                with act.Fori(1, E * (NBLK - 1) + 1) as b:
                    act.wait_ge(more_turn, 2 * b - 1)
                    for z_ in range(2):
                        i_ = act.activation(xf[:, 4 * z_:4 * z_ + 4, :], ps[:, 6 + z_, :].rearrange("p (k n) -> p k n", k=4), ACT.Copy)
                    i_.then_inc(more_xf, 1)
                    act.wait_ge(more_act, 2 * b - 1)
                    act.activation(sg[:, :], gm[:, :], ACT.Sigmoid, scale=ALPHA).then_inc(more_sig, 1)
                    act.wait_ge(more_turn, 2 * b)
                    for z_ in range(2):
                        i_ = act.activation(af[:, 4 * z_:4 * z_ + 4, :], ps[:, 6 + z_, :].rearrange("p (k n) -> p k n", k=4), ACT.Copy)
                    i_.then_inc(more_af, 1)
                    act.wait_ge(more_dn, b)
                    for z_ in range(2):
                        i_ = act.activation(yo[:, 512 * z_:512 * z_ + 512], ps[:, 4 + z_, :], ACT.Copy)
                    i_.then_inc(more_y, 1)

        def routing_pe(pe):
            for t in range(NT):
                pe.wait_ge(hf_done, t + 1)
                if t >= 2:
                    pe.wait_ge(hfT_act, t - 1)
                    pe.wait_ge(hfT_dve, t - 1)
                for k in range(KD):
                    mm = pe.transpose(ps[:, SIDE + 2 * (t % 2) + k // 4, (k % 4) * P:(k % 4 + 1) * P], hf[:, t, k * P:(k + 1) * P], ident[:, :])
                mm.then_inc(hf_turned, 1)
                pe.wait_ge(hfT_act, t + 1)
                pe.wait_ge(hfT_dve, t + 1)
                if t == 0:
                    pe.wait_ge(wr_in, 16)
                for k in range(KD):
                    pe.matmul(ps[:, LOGIT + t, 0:E], hfT[:, k, t * P:(t + 1) * P], wr[:, k, :], start=(k == 0), stop=False)
                pe.matmul(ps[:, LOGIT + t, 0:E], ones[0:1, :], bro, start=False, stop=True).then_inc(logit_done, 1)
            pe.wait_ge(msk_ready, 1)
            for t in range(NT):
                for u in range(t + 1):
                    pe.matmul(ps[:, ROUTE, t * E:(t + 1) * E], (before if u == t else onesb)[:, :], mskb[:, u, :],
                              start=(u == 0), stop=(u == t))
            for u in range(NT):
                mm = pe.matmul(ps[:, ROUTE, NT * E:(NT + 1) * E], onesb[:, :], mskb[:, u, :], start=(u == 0), stop=(u == NT - 1))
            mm.then_inc(pos_done, 1)

            def turn_x(e):
                pe.wait_ge(xg_in, (e + 1) * 16)
                if not (isinstance(e, int) and e <= 1):
                    pe.wait_ge(a_split, e - 1)
                for k in range(KD):
                    mm = pe.transpose(ps[:, 6 + k // 4, (k % 4) * P:(k % 4 + 1) * P], xg[:, k * P:(k + 1) * P], ident[:, :])
                mm.then_inc(x_turned, 1)

            def turn_a(e):
                pe.wait_ge(ac_done, e + 1)
                pe.wait_ge(x_split, e + 2)
                for k in range(KD):
                    mm = pe.transpose(ps[:, 6 + k // 4, (k % 4) * P:(k % 4 + 1) * P], ac[:, k * P:(k + 1) * P], ident[:, :])
                mm.then_inc(a_turned, 1)

            def run_gu(e):
                if not (isinstance(e, int) and e == 0):
                    pe.wait_ge(gu_free, e * 2)
                for n in range(4):
                    pe.matmul(ps[:, n, :], pick[:, bass.ds(e * P, P)], ebias[:, 512 * n:512 * n + 512], start=True, stop=False)
                pe.wait_ge(x_split, e + 1)
                for k in range(GU):
                    pe.wait_ge(w_lo, at(e, k) + 1)
                    for z_, (x_, w_) in enumerate(((xh, eh), (xh, el), (xl, eh))):
                        for n in range(4):
                            mm = pe.matmul(ps[:, n, :], x_[:, k, :], w_[:, k % BUFS, 512 * n:512 * n + 512], start=False,
                                           stop=(k == GU - 1 and z_ == 2))
                    mm.then_inc(e_used, 1)

            def run_dn(e, i, first):
                if not (isinstance(e, int) and e == 0):
                    pe.wait_ge(dn_free, e)
                for n in range(2):
                    pe.matmul(ps[:, 4 + n, :], pick[:, bass.ds(e * P, P)], ebias[:, 2 * FF + 512 * n:2 * FF + 512 * n + 512], start=True, stop=False)
                pe.wait_ge(a_split, e + 1)
                for m in range(DN):
                    pe.wait_ge(w_lo, at(i, first + m) + 1)
                    for kk in range(2):
                        for z_, (x_, w_) in enumerate(((ah, eh), (ah, el), (al, eh))):
                            for n in range(2):
                                mm = pe.matmul(ps[:, 4 + n, :], x_[:, 2 * m + kk, :],
                                               w_[:, m % BUFS, FF * kk + 512 * n:FF * kk + 512 * n + 512], start=False,
                                               stop=(m == DN - 1 and kk == 1 and z_ == 2))
                    mm.then_inc(e_used, 1)

            def body(e):
                if e is None:
                    run_dn(E - 1, E, 0)
                    return
                run_gu(e)
                turn_x(e + 1)
                if not (isinstance(e, int) and e == 0):
                    run_dn(e - 1, e, GU)
                turn_a(e)

            pe.wait_ge(most_ready, 1)
            turn_x(0)
            pe.wait_ge(picks_ready, 1)
            pe.wait_ge(ebias_ready, 1)
            iterations(pe, body)
            pe.wait_ge(y_out, 16 * E)
            many = pe.value_load(most[0:1, 0:1], min_val=0, max_val=SEQ)
            with pe.If(many > BLK):
                with pe.Fori(1, NBLK) as j:
                    with pe.Fori(0, E) as e:
                        b = j * E + e - (E - 1)
                        pe.wait_ge(more_x, b * 16)
                        for k in range(KD):
                            mm = pe.transpose(ps[:, 6 + k // 4, (k % 4) * P:(k % 4 + 1) * P], xg[:, k * P:(k + 1) * P], ident[:, :])
                        mm.then_inc(more_turn, 1)
                        for n in range(4):
                            pe.matmul(ps[:, n, :], pick[:, bass.ds(e * P, P)], ebias[:, 512 * n:512 * n + 512], start=True, stop=False)
                        pe.wait_ge(more_xf, b)
                        pe.wait_ge(more_w, b * PER * 16)
                        for k in range(GU):
                            for n in range(4):
                                mm = pe.matmul(ps[:, n, :], xf[:, k, :], wide[:, k, 512 * n:512 * n + 512], start=False, stop=(k == GU - 1))
                        mm.then_inc(more_gu, 1)
                        pe.wait_ge(more_act, 2 * b)
                        for k in range(KD):
                            mm = pe.transpose(ps[:, 6 + k // 4, (k % 4) * P:(k % 4 + 1) * P], ac[:, k * P:(k + 1) * P], ident[:, :])
                        mm.then_inc(more_turn, 1)
                        for n in range(2):
                            pe.matmul(ps[:, 4 + n, :], pick[:, bass.ds(e * P, P)], ebias[:, 2 * FF + 512 * n:2 * FF + 512 * n + 512], start=True, stop=False)
                        pe.wait_ge(more_af, b)
                        for k in range(KD):
                            for n in range(2):
                                mm = pe.matmul(ps[:, 4 + n, :], af[:, k, :], ring[:, k // 2, FF * (k % 2) + 512 * n:FF * (k % 2) + 512 * n + 512],
                                               start=False, stop=(k == KD - 1))
                        mm.then_inc(more_dn, 1)

        def routing_dve(dve, link, chain, newton):
            dve.wait_ge(squared2, NT)
            dve.tensor_scalar(m2, ss2, 1.0 / D, EPS, ALU.mult, ALU.add).then_inc(m2_ready, 1)
            dve.wait_ge(m2_ready, 1)
            dve.wait_ge(r2_ready, 1)
            newton(r2, m2, t2)
            for t in range(NT):
                dve.scalar_tensor_tensor(hf[:, t, :], x2[:, t, :], r2[:, t:t + 1], gbc[:, :], ALU.mult, ALU.mult).then_inc(hf_done, 1)
            dve.wait_ge(rmade, 1)
            dve.tensor_copy(iotaf, iotai[:, :])
            for t in range(NT):
                dve.wait_ge(hf_turned, t + 1)
                dve.tensor_copy(hfT[:, 4:8, t * P:(t + 1) * P], ps[:, SIDE + 2 * (t % 2) + 1, :].rearrange("p (k n) -> p k n", k=4)).then_inc(hfT_dve, 1)
            for t in range(NT):
                dve.wait_ge(logit_done, t + 1)
                link(dve.tensor_copy(lg[:, t, :], ps[:, LOGIT + t, 0:E]))
                link(dve.max(v8[:, t, :], lg[:, t, :]))
                link(dve.max_index(i8[:, t, :], v8[:, t, :], lg[:, t, :]))
            dve.tensor_scalar(gneg, v8[:, :, 0], -1.0, None, ALU.mult).then_inc(best_ready, 1)
            link(dve.tensor_copy(i8f[:, :, :], i8[:, :, :]))
            for t in range(NT):
                for k in range(TOPK):
                    i_ = dve.tensor_scalar(oneh[:, t * TOPK + k, :], iotaf, i8f[:, t, k:k + 1], None, ALU.is_equal)
            link(i_)
            by_k = oneh.rearrange("p (t k) e -> p k t e", k=TOPK)
            link(dve.tensor_tensor(msk, by_k[:, 0], by_k[:, 1], ALU.add))
            link(dve.tensor_tensor(msk, msk, by_k[:, 2], ALU.add))
            dve.tensor_tensor(mskb[:, :, :], msk, by_k[:, 3], ALU.add).then_inc(msk_ready, 1)
            dve.wait_ge(pos_done, 1)
            link(dve.tensor_copy(posf, ps[:, ROUTE, 0:NT * E].rearrange("p (t e) -> p t e", e=E)))
            for t in range(NT):
                for k in range(TOPK):
                    x_ = t * TOPK + k
                    link(dve.tensor_tensor_reduce(junk[:, 0:E], oneh[:, x_, :], posf[:, t, :], 1.0, 0.0, ALU.mult, ALU.add, pk[:, x_:x_ + 1]))
            link(dve.tensor_scalar(jj, pk, float(BLK), None, ALU.is_ge))
            for b in range(2, NBLK):
                link(dve.tensor_scalar(tif, pk, float(BLK * b), None, ALU.is_ge))
                link(dve.tensor_tensor(jj, jj, tif, ALU.add))
            link(dve.tensor_scalar(tif, pk, float(COLS), None, ALU.mult))
            link(dve.scalar_tensor_tensor(tif, jj, float(E - COLS * BLK), tif, ALU.mult, ALU.add))
            link(dve.tensor_tensor(tif.rearrange("p (t k) -> p t k", k=TOPK), i8f[:, :, 0:TOPK],
                                   tif.rearrange("p (t k) -> p t k", k=TOPK), ALU.add))
            dve.tensor_copy(ti[:, :], tif).then_inc(ti_ready, 1)
            link(dve.tensor_reduce(junk[:, 0:1], ps[:, ROUTE, NT * E:(NT + 1) * E], AX.X, ALU.max))
            dve.tensor_copy(most[:, 0:1], junk[:, 0:1]).then_inc(most_ready, 1)
            dve.wait_ge(gexp_done, 1)
            link(dve.reciprocal(grec, gsum))
            for t in range(NT):
                i_ = dve.tensor_scalar(gw[:, t, :], gw[:, t, :], grec[:, t:t + 1], None, ALU.mult)
            link(i_)
            dve.wait_ge(braw_in, 16 * 6)
            link(dve.tensor_copy(ebias[:, :], braw[:, :]))
            for q in (1, 2):
                for u in range(q, 3):
                    i_ = dve.tensor_tensor(braw[u * E:(u + 1) * E, :], braw[u * E:(u + 1) * E, :], ebias[u * E:(u + 1) * E, :], ALU.subtract)
                link(i_)
                for u in range(q, 3):
                    i_ = dve.tensor_copy(ebias[u * E:(u + 1) * E, :], braw[u * E:(u + 1) * E, :])
                if q == 1:
                    link(i_)
            i_.then_inc(ebias_ready, 1)
            dve.wait_ge(slot_in, 16)
            dve.tensor_scalar(tok[:, :], row[:, :], TOPK.bit_length() - 1, None, ALU.logical_shift_right).then_inc(tok_ready, 1)

            def lo_split(e, n):
                dve.wait_ge(w_hi, at(e, n) + 1)
                dve.tensor_tensor(el[:, n % BUFS, :], ring[:, n % SLOTS, :], eh[:, n % BUFS, :].bitcast(F32), ALU.subtract).then_inc(w_lo, 1)

            def x_lo(e):
                dve.wait_ge(xh_done, e + 1)
                for z_ in range(2):
                    i_ = dve.tensor_tensor(xl[:, 4 * z_:4 * z_ + 4, :], ps[:, 6 + z_, :].rearrange("p (k n) -> p k n", k=4),
                                           xh[:, 4 * z_:4 * z_ + 4, :].bitcast(F32), ALU.subtract)
                i_.then_inc(x_split, 1)

            def a_lo(e):
                dve.wait_ge(ah_done, e + 1)
                for z_ in range(2):
                    i_ = dve.tensor_tensor(al[:, 4 * z_:4 * z_ + 4, :], ps[:, 6 + z_, :].rearrange("p (k n) -> p k n", k=4),
                                           ah[:, 4 * z_:4 * z_ + 4, :].bitcast(F32), ALU.subtract)
                i_.then_inc(a_split, 1)

            def clamp_gate(e):
                dve.wait_ge(e_used, e * PER + (GU - DN) if not (isinstance(e, int) and e == 0) else GU)
                dve.tensor_scalar(gm[:, :].rearrange("p (b n) -> p b n", b=2), ps[:, 0:2, :], LIMIT, None, ALU.min).then_inc(gm_done, 1)

            def clip_up(e):
                dve.tensor_scalar(lc[:, :].rearrange("p (b n) -> p b n", b=2), ps[:, 2:4, :], -LIMIT, LIMIT, ALU.max, ALU.min).then_inc(gu_free, 2)
                dve.wait_ge(gu_free, (e + 1) * 2)
                dve.wait_ge(gm_done, e + 1)
                dve.scalar_tensor_tensor(lc[:, :], lc[:, :], 1.0, gm[:, :], ALU.add, ALU.mult).then_inc(lin_done, 1)

            def finish_act(e):
                dve.wait_ge(lin_done, e + 1)
                dve.wait_ge(sg_done, e + 1)
                dve.tensor_tensor(ac[:, :], lc[:, :], sg[:, :], ALU.mult).then_inc(ac_done, 1)

            def body(e):
                if e is None:
                    for m in range(DN):
                        lo_split(E, m)
                    a_lo(E - 1)
                    return
                first = isinstance(e, int) and e == 0
                for n in range(GU if first else PER):
                    lo_split(e, n)
                    if n == BUFS - 1 and not first:
                        a_lo(e - 1)
                    if n == PER - 2:
                        clamp_gate(e)
                if first:
                    clamp_gate(0)
                clip_up(e)
                x_lo(e + 1)
                finish_act(e)

            x_lo(0)
            iterations(dve, body)
            dve.wait_ge(y_out, 16 * E)
            many = dve.value_load(most[0:1, 0:1], min_val=0, max_val=SEQ)
            with dve.If(many > BLK):
                with dve.Fori(1, E * (NBLK - 1) + 1) as b:
                    dve.wait_ge(more_gu, b)
                    dve.tensor_scalar(gm[:, :].rearrange("p (b n) -> p b n", b=2), ps[:, 0:2, :], LIMIT, None, ALU.min).then_inc(more_act, 1)
                    dve.tensor_scalar(lc[:, :].rearrange("p (b n) -> p b n", b=2), ps[:, 2:4, :], -LIMIT, LIMIT, ALU.max, ALU.min).then_inc(more_lin, 1)
                    dve.wait_ge(more_act, 2 * b - 1)
                    dve.wait_ge(more_lin, 2 * b - 1)
                    dve.scalar_tensor_tensor(lc[:, :], lc[:, :], 1.0, gm[:, :], ALU.add, ALU.mult).then_inc(more_lin, 1)
                    dve.wait_ge(more_lin, 2 * b)
                    dve.wait_ge(more_sig, b)
                    dve.tensor_tensor(ac[:, :], lc[:, :], sg[:, :], ALU.mult).then_inc(more_act, 1)
            for t in range(NT):
                dve.wait_ge(yg_in[t], 16)
                for k in range(TOPK):
                    i_ = dve.scalar_tensor_tensor(x2[:, t, :], yg[:, t, k, :], gw[:, t, k:k + 1], x2[:, t, :], ALU.mult, ALU.add)
                    if k < TOPK - 1:
                        link(i_)
                i_.then_inc(summed, 1)

        def routing_pool(pool):
            count = [0]

            def after(ins):
                count[0] += 1
                ins.then_inc(pool_step, 1)
                pool.wait_ge(pool_step, count[0])

            pool.wait_ge(gl_done, KD)
            pool.dma_start(wr[:, :, :], a["w_router"][0].rearrange("(k p) e -> p k e", p=P)).then_inc(wr_in, 16)
            after(pool.iota(iotai[:, :], pattern=[[1, E]], base=0, channel_multiplier=0))
            after(pool.iota(rows[:, :], pattern=[[TOPK * P, NT], [1, TOPK]], base=0, channel_multiplier=TOPK))
            pool.iota(never[:, :], pattern=[[TOPK * P, COLS]], base=NEVER, channel_multiplier=TOPK).then_inc(rmade, 1)
            pool.wait_ge(rmade, 1)
            pool.dma_start(slot_d.rearrange("(p c) o -> p (c o)", p=P), never[:, :]).then_inc(slot_set, 16)
            after(pool.memset(pick[:, :], 1.0))
            pick3 = pick[:, :].rearrange("p (e n) -> p e n", n=P)
            for q in range(3):
                part = pick3[q * E:(q + 1) * E]
                i_ = pool.affine_select(out=part, in_=part, compare_op=ALU.is_equal, fill=0.0, base=0, pattern=[[-1, E], [0, P]],
                                        channel_multiplier=1)
                if q < 2:
                    after(i_)
            i_.then_inc(picks_ready, 1)
            pool.wait_ge(picks_ready, 1)
            pool.wait_ge(unit_done, USED[NM - 1])
            for q in range(3):
                pool.dma_start(braw[q * E:(q + 1) * E, 0:2 * FF], a["b_gate_up"][0]).then_inc(braw_in, 16)
                pool.dma_start(braw[q * E:(q + 1) * E, 2 * FF:3 * FF], a["b_down"][0]).then_inc(braw_in, 16)
            pool.wait_ge(slot_set, 16)
            pool.wait_ge(ti_ready, 1)
            for x_ in range(NT * TOPK):
                pool.indirect_dma_start(slot_d[:, :], bass.IndirectOffsetOnAxis(ap=ti[:, x_:x_ + 1], axis=0), rows[:, x_:x_ + 1],
                                        None).then_inc(slot_out, 16)
            pool.wait_ge(slot_out, 16 * NT * TOPK)
            pool.dma_start(row[:, :], slot_d.rearrange("(p c) o -> p (c o)", p=P)).then_inc(slot_in, 16)
            pool.wait_ge(hf_out, 16 * NT)
            pool.wait_ge(hf_turned, NT)
            after(pool.memset(xg[:, :], 0.0))
            pool.wait_ge(tok_ready, 1)


            def gather(column, into):
                after_now(pool.tensor_copy(now[:, 0:1], tok[:, bass.ds(column, 1)]))
                pool.indirect_dma_start(xg[:, :], None, hf_d[:, :], bass.IndirectOffsetOnAxis(ap=now[:, 0:1], axis=0),
                                        bounds_check=column + (SEQ - 1), oob_is_err=False).then_inc(into, 16)

            def scatter(column, into):
                after_now(pool.tensor_copy(now[:, 1:2], row[:, bass.ds(column, 1)]))
                pool.indirect_dma_start(y_d[:, :], bass.IndirectOffsetOnAxis(ap=now[:, 1:2], axis=0), yo[:, :], None,
                                        bounds_check=column + (SEQ * TOPK - 1), oob_is_err=False).then_inc(into, 16)

            def after_now(ins):
                ins.then_inc(pool_now, 1)
                pool.wait_ge(pool_now, turn[0])

            turn = [1]
            gather(0, xg_in)

            def body(e):
                if e is None:
                    turn[0] = 2 * E
                    pool.wait_ge(dn_free, E - 1)
                    pool.wait_ge(y_out, 16 * (E - 2))
                    scatter(E - 2, y_out)
                    pool.wait_ge(dn_free, E)
                    turn[0] = 2 * E + 1
                    pool.wait_ge(y_out, 16 * (E - 1))
                    scatter(E - 1, y_out)
                    return
                early = isinstance(e, int) and e < 2
                if not early:
                    turn[0] = 2 * e
                    pool.wait_ge(dn_free, e - 1)
                    if not (isinstance(e, int) and e == 2):
                        pool.wait_ge(y_out, (e - 2) * 16)
                    scatter(e - 2, y_out)
                    turn[0] = 2 * e + 1
                else:
                    turn[0] = e + 2
                pool.wait_ge(x_turned, e + 1)
                gather(e + 1, xg_in)

            iterations(pool, body)

            pool.wait_ge(y_out, 16 * E)
            pool.wait_ge(most_ready, 1)
            many = pool.value_load(most[0:1, 0:1], min_val=0, max_val=SEQ)
            with pool.If(many > BLK):
                with pool.Fori(E, E * NBLK) as b:
                    turn[0] = b * 2 + 2
                    pool.wait_ge(y_out, b * 16)
                    gather(b, more_x)
                    turn[0] = b * 2 + 3
                    pool.wait_ge(more_y, b - (E - 1))
                    scatter(b, y_out)

        block = ctx.enter_context(nc.Block())

        @block.sync
        def _(sp_):
            for n, (g, t) in enumerate(TILES):
                s = n % SLOTS_MIX
                if n >= SLOTS_MIX:
                    sp_.wait_ge(w_lo, n - SLOTS_MIX + 1)
                sp_.dma_start(ring[:, s, :].rearrange("p (k n) -> p k n", k=4), weight_source(g, t)).then_inc(w_in[s], 16)
            if not stop_after_mixer:
                experts_sync(sp_)

        @block.scalar
        def _(act):
            for dst, src in small_loads:
                act.dma_start(dst, src).then_inc(small_in, 16)
            for r in range(NT + MT):
                act.wait_ge(xm_in[r], 16)
                if r:
                    act.wait_ge(squared, r)
                act.activation(sqd[:, :], xm[:, r, :], ACT.Square, accum_out=ssx[:, r:r + 1]).then_inc(squared, 1)
            act.wait_ge(mean_ready, 1)
            act.activation(rx, mx_, ACT.Ln).then_inc(act_step, 1)
            act.wait_ge(act_step, 1)
            act.activation(rx, rx, ACT.Exp, scale=-0.5).then_inc(root_ready, 1)
            act.wait_ge(small_in, 16 * len(small_loads))
            for i, (which, k) in enumerate(TURNS):
                gain, hi, n = (memg, mh, MEM) if which == "m" else (mixg, hh, SEQ)
                act.wait_ge(turned, i + 1)
                act.activation(hi[:, k, :], ps[:, i % 8, 0:n], ACT.Copy, scale=gain[:, k:k + 1]).then_inc(h_hi, 1)
            steps_seen = 1
            for step in STEPS:
                kind, x = step[0], step[1:]
                if kind == "split":
                    n, = x
                    s = n % SLOTS_MIX
                    act.wait_ge(w_in[s], 16 * (n // SLOTS_MIX + 1))
                    if n >= 2:
                        act.wait_ge(unit_done, USED[n - 2])
                    act.activation(split(n)[0], ring[:, s, :], ACT.Copy).then_inc(w_hi, 1)
                elif kind == "save" and BY_ACT(x[0]):
                    g, c = x
                    act.wait_ge(unit_done, SUMMED[x])
                    if g in NORMED:
                        y = NORMS[x] - 1
                        if y >= 2:
                            act.wait_ge(ssum_done, y - 1)
                        act.activation(nsq[:, y % 2, 0:GROUPS[g][1]], chunk(g, c), ACT.Square).then_inc(nsq_ready, 1)
                        act.activation(normed_chunk(g, c), chunk(g, c), ACT.Copy).then_inc(saved_act, 1)
                    elif g in LATE:
                        place, had = LATE[g]
                        act.wait_ge(saved_dve, SAVED_DVE[had, c])
                        act.activation(gate[:, place, c, :], chunk(g, c), ACT.Sigmoid).then_inc(saved_act, 1)
                    else:
                        dst = {"mv": vm, "v": v, "cc": cu}[g][:, c, :] if g in ("mv", "v", "cc") else gate[:, EARLY_GATES.index(g), c, :]
                        act.activation(dst, chunk(g, c), ACT.Copy).then_inc(saved_act, 1)
                elif kind == "save" and x[0][:2] == "b2":
                    g, c = x
                    d = 4 * int(g[2]) + c
                    act.wait_ge(unit_done, SUMMED["b11", 3])
                    act.wait_ge(acc_done, d + 1)
                    act.activation(gh[:, d, :], acc[:, d, :], ACT.Copy).then_inc(gh_done, 1)
                elif kind == "norm":
                    g, c = x
                    y = NORMS[x] - 1
                    n = GROUPS[g][1]
                    act.wait_ge(nm_ready, y + 1)
                    act.activation(ny[:, y % 2, 0:n], nm_[:, y % 2, 0:n], ACT.Ln).then_inc(act_step, 1)
                    steps_seen += 1
                    act.wait_ge(act_step, steps_seen)
                    act.activation(ny[:, y % 2, 0:n], ny[:, y % 2, 0:n], ACT.Exp, scale=-0.5).then_inc(ny_ready, 1)
                elif kind == "msoft":
                    h, = x
                    act.wait_ge(mneg_ready, h + 1)
                    if h:
                        act.wait_ge(mt_done, h)
                    for t in range(NT):
                        e_ = act.activation(pm[:, t, :], ps[:, 4 + t // 2, (t % 2) * MEM:(t % 2 + 1) * MEM], ACT.Exp,
                                            bias=mneg_[:, t:t + 1], scale=SCALE_M, accum_out=msum[:, t:t + 1])
                    e_.then_inc(mexp_done, 1)
                elif kind == "mturn":
                    h, = x
                    act.wait_ge(mt_done, h + 1)
                    if h:
                        act.wait_ge(mo_done, h)
                    act.activation(pT[:, 0, :], ps[:, 6, :], ACT.Copy).then_inc(mt_act, 1)
                elif kind == "soft":
                    h, = x
                    act.wait_ge(z_done, h + 1)
                    if h:
                        act.wait_ge(sp_done, 2 * h)
                    for b, (lo, hi) in (((2, 3), (OFF[2], PACKED)), ((0, 1), (0, OFF[2]))):
                        for i in b:
                            e_ = act.activation(we[:, OFF[i]:OFF[i] + WIDTH[i]], ps[:, 4 + i, P * i:SEQ], ACT.Abs)
                        e_.then_inc(act_step, 1)
                        steps_seen += 1
                        act.wait_ge(act_step, steps_seen)
                        act.activation(we[:, lo:hi], we[:, lo:hi], ACT.Exp, scale=-1.0).then_inc(act_step, 1)
                        steps_seen += 1
                        act.wait_ge(act_step, steps_seen)
                        act.activation(we[:, lo:hi], we[:, lo:hi], ACT.Ln, bias=1.0).then_inc(log_done, 1)
                elif kind == "between":
                    h, = x
                    if h:
                        act.wait_ge(av_done, h)
                    for n, i in enumerate(reversed(range(NT))):
                        act.wait_ge(c_done, NT * h + n + 1)
                        act.activation(w[:, OFF[i]:OFF[i] + WIDTH[i]], ps[:, 4 + i, P * i:SEQ], ACT.Exp).then_inc(w_done, 1)
                elif kind == "osplit":
                    i, = x
                    act.wait_ge(o_saved, SBH)
                    act.wait_ge(saved_dve, SAVED_DVE["cb", 3])
                    act.activation(oh[i][:, :, :], (osb, oc, om)[i][:, :, :], ACT.Copy).then_inc(oh_done, 1)
                elif kind == "sig":
                    i, = x
                    act.wait_ge(saved_act, SAVED_ACT[EARLY_GATES[i], 3])
                    act.activation(gate[:, i], gate[:, i], ACT.Sigmoid).then_inc(sig_done, 1)
            if not stop_after_mixer:
                routing_act(act, steps_seen)

        @block.tensor
        def _(pe):
            pe.wait_ge(made, MADE)
            pe.wait_ge(made_dve, 1)
            pe.wait_ge(scaled, NT + MT)
            for i, (which, k) in enumerate(TURNS):
                if i >= 8:
                    pe.wait_ge(h_lo, i - 7)
                first, n = (T0, MT) if which == "m" else (0, NT)
                for r in range(n):
                    mm = pe.transpose(ps[:, i % 8, r * P:(r + 1) * P], xm[:, first + r, k * P:(k + 1) * P], ident[:, :])
                mm.then_inc(turned, 1)
            pe.wait_ge(h_lo, len(TURNS))
            for step in STEPS:
                kind, x = step[0], step[1:]
                if kind == "unit":
                    g, t, c = x
                    n = NUMBER[g, t]
                    if c == 0:
                        pe.wait_ge(w_lo, n + 1)
                    if t == 0 and FREED_BY[g, c]:
                        by = FREED_BY[g, c]
                        if BY_ACT(by[0]):
                            pe.wait_ge(saved_act, SAVED_ACT[by])
                        else:
                            pe.wait_ge(saved_dve, SAVED_DVE[by])
                    if g[0] == "b":
                        pe.wait_ge(osplit_done, int(g[1]) + 1)
                    if g[0] == "o":
                        pe.wait_ge(gl_done, 4 * t + 4)
                    hi, lo = operands(g)
                    whi, wlo = (z_.rearrange("p (k n) -> p k n", k=4) for z_ in split(n))
                    last = GROUPS[g][0] - 1
                    for k in range(4):
                        for z_, (av_, wv_) in enumerate(((hi, whi), (hi, wlo), (lo, whi))):
                            if g in TOKEN_MAJOR:
                                lhs, rhs = av_[:, 4 * t + k, c * P:(c + 1) * P], wv_[:, k, :]
                            else:
                                lhs, rhs = wv_[:, k, c * P:(c + 1) * P], av_[:, 4 * t + k, :]
                            mm = pe.matmul(chunk(g, c), lhs, rhs, start=(t == 0 and k == 0 and z_ == 0),
                                           stop=(t == last and k == 3 and z_ == 2))
                    mm.then_inc(unit_done, 1)
                elif kind == "ssum":
                    y = NORMS[x] - 1
                    n = GROUPS[x[0]][1]
                    pe.wait_ge(nsq_ready, y + 1)
                    if y >= 4:
                        pe.wait_ge(nm_ready, y - 3)
                    pe.matmul(ps[:, 4 + y % 4, 0:n], (halves if x[0] in "qk" else ones)[:, :], nsq[:, y % 2, 0:n],
                              start=True, stop=True).then_inc(ssum_done, 1)
                elif kind == "mscore":
                    h, = x
                    if h == 0:
                        pe.wait_ge(normed, len(NORMS))
                    else:
                        pe.wait_ge(om_saved, h)
                    for t in range(NT):
                        mm = pe.matmul(ps[:, 4 + t // 2, (t % 2) * MEM:(t % 2 + 1) * MEM], qm[:, h, t * P:(t + 1) * P],
                                       km[:, h, :], start=True, stop=True)
                    mm.then_inc(ms_done, 1)
                elif kind == "mturn":
                    h, = x
                    pe.wait_ge(mprob_ready, h + 1)
                    if h:
                        pe.wait_ge(mt_act, h)
                        pe.wait_ge(mt_dve, h)
                    for m in range(MT):
                        for t in range(NT):
                            mm = pe.transpose(ps[:, 6 + m, t * P:(t + 1) * P], pm[:, t, m * P:(m + 1) * P], ident[:, :])
                    mm.then_inc(mt_done, 1)
                elif kind == "mout":
                    h, = x
                    pe.wait_ge(mt_act, h + 1)
                    pe.wait_ge(mt_dve, h + 1)
                    pe.wait_ge(saved_act, SAVED_ACT["mv", MT - 1])
                    for m in range(MT):
                        mm = pe.matmul(ps[:, 4, :], vm[:, m, h * P:(h + 1) * P], pT[:, m, :], start=(m == 0), stop=(m == MT - 1))
                    mm.then_inc(mo_done, 1)
                elif kind == "z":
                    h, = x
                    lo = DH * (h % 2)
                    if h == 0:
                        pe.wait_ge(om_saved, MH)
                    else:
                        pe.wait_ge(o_saved, h)
                    for i in range(NT):
                        pe.matmul(ps[:, 4 + i, P * i:SEQ], kT[lo:lo + DH, h // 2, P * i:P * (i + 1)],
                                  qT[lo:lo + DH, h // 2, P * i:SEQ], start=True, stop=True)
                        mm = pe.matmul(ps[:, 4 + i, P * i:P * (i + 1)], identb[:, :], maskb[:, :], start=False, stop=True,
                                       skip_group_check=True)
                    mm.then_inc(z_done, 1)
                elif kind == "between":
                    h, = x
                    for n, i in enumerate(reversed(range(NT))):
                        pe.wait_ge(spl_done, 2 * h + (1 if i >= 2 else 2))
                        for j in range(i, NT):
                            for part in (sph, spl):
                                mm = pe.matmul(ps[:, 4 + i, P * j:SEQ], (down if j == i else minus)[:, :],
                                               part[:, OFF[j]:OFF[j] + WIDTH[j]], start=False, stop=True,
                                               skip_group_check=True)
                        mm.then_inc(c_done, 1)
                elif kind == "av":
                    h, = x
                    lo = DH * (h % 2)
                    pe.wait_ge(w_done, NT * (h + 1))
                    pe.wait_ge(saved_act, SAVED_ACT["v", NT - 1])
                    for i in range(NT):
                        mm = pe.matmul(ps[lo:lo + DH, 4, P * i:SEQ], v[:, i, DH * h:DH * (h + 1)],
                                       w[:, OFF[i]:OFF[i] + WIDTH[i]], start=(i == 0), stop=True,
                                       skip_group_check=True)
                    mm.then_inc(av_done, 1)
            if not stop_after_mixer:
                routing_pe(pe)

        @block.vector
        def _(dve):
            chain = [0]

            def link(ins):
                chain[0] += 1
                ins.then_inc(dve_step, 1)
                dve.wait_ge(dve_step, chain[0])

            dve.wait_ge(made, MADE)
            dve.memset(minus[:, :].bitcast(F32), -1.0)
            dve.tensor_copy(down[:, :], downf[:, :]).then_inc(made_dve, 1)

            def newton(r, m, t, mult_last=None):
                link(dve.scalar_tensor_tensor(t, r, -0.5, r, ALU.mult, ALU.mult))
                link(dve.tensor_tensor(t, t, m, ALU.mult))
                link(dve.scalar_tensor_tensor(r, t, 1.5, r, ALU.add, ALU.mult))

            dve.wait_ge(squared, NT + MT)
            dve.tensor_scalar(mx_, ssx, 1.0 / D, EPS, ALU.mult, ALU.add).then_inc(mean_ready, 1)
            dve.wait_ge(small_in, 16 * len(small_loads))
            link(dve.tensor_scalar(qg, qg, DH ** -0.5, None, ALU.mult))
            dve.wait_ge(mean_ready, 1)
            dve.wait_ge(root_ready, 1)
            newton(rx, mx_, tx)
            for r in range(NT + MT):
                dve.tensor_scalar(xm[:, r, :], xm[:, r, :], rx[:, r:r + 1], None, ALU.mult).then_inc(scaled, 1)
            for i, (which, k) in enumerate(TURNS):
                gain, hi, lo, n = (memg, mh, ml, MEM) if which == "m" else (mixg, hh, hl, SEQ)
                dve.wait_ge(h_hi, i + 1)
                dve.scalar_tensor_tensor(lo[:, k, :], ps[:, i % 8, 0:n], gain[:, k:k + 1], hi[:, k, :].bitcast(F32),
                                         ALU.mult, ALU.subtract).then_inc(h_lo, 1)
            for step in STEPS:
                kind, x = step[0], step[1:]
                if kind == "split":
                    n, = x
                    dve.wait_ge(w_hi, n + 1)
                    hi, lo = split(n)
                    dve.tensor_tensor(lo, ring[:, n % SLOTS_MIX, :], hi.bitcast(F32), ALU.subtract).then_inc(w_lo, 1)
                elif kind == "save" and not BY_ACT(x[0]):
                    g, c = x
                    dve.wait_ge(unit_done, SUMMED[x])
                    if g == "cx":
                        dve.wait_ge(saved_act, SAVED_ACT["cc", c])
                        dve.tensor_tensor(cu[:, c, :], chunk(g, c), cu[:, c, :], ALU.mult).then_inc(saved_dve, 1)
                        dve.wait_ge(saved_dve, SAVED_DVE[x])
                        link(dve.tensor_scalar(oc[:, c, :], cu[:, c, :], taps[:, 8 + c:9 + c], None, ALU.mult))
                        link(dve.scalar_tensor_tensor(oc[:, c, 1:SEQ], cu[:, c, 0:SEQ - 1], taps[:, 4 + c:5 + c],
                                                      oc[:, c, 1:SEQ], ALU.mult, ALU.add))
                        link(dve.scalar_tensor_tensor(oc[:, c, 2:SEQ], cu[:, c, 0:SEQ - 2], taps[:, c:c + 1],
                                                      oc[:, c, 2:SEQ], ALU.mult, ALU.add))
                    elif g == "cb":
                        dve.tensor_tensor(oc[:, c, :], chunk(g, c), oc[:, c, :], ALU.mult).then_inc(saved_dve, 1)
                    elif g[0] == "b":
                        i, d = int(g[1]), 4 * int(g[2]) + c
                        late = [q for q in LATE if PLACE[g] == LATE[q][0] and q[1:] == g[1:]]
                        if late:
                            dve.wait_ge(saved_act, SAVED_ACT[late[0], c])
                        else:
                            dve.wait_ge(sig_done, EARLY_GATES.index("g" + g[1:]) + 1)
                        if i == 0:
                            dve.tensor_tensor(acc[:, d, :], chunk(g, c), gate[:, PLACE[g], c, :], ALU.mult).then_inc(saved_dve, 1)
                        else:
                            dve.tensor_tensor(tmp[:, c % 2, :], chunk(g, c), gate[:, PLACE[g], c, :], ALU.mult).then_inc(saved_dve, 1)
                            dve.wait_ge(saved_dve, SAVED_DVE[x])
                            add = dve.tensor_tensor(acc[:, d, :], acc[:, d, :], tmp[:, c % 2, :], ALU.add)
                            if i == 1:
                                link(add)
                            else:
                                add.then_inc(acc_done, 1)
                                dve.wait_ge(gh_done, d + 1)
                                dve.tensor_tensor(gl[:, d, :], acc[:, d, :], gh[:, d, :].bitcast(F32), ALU.subtract).then_inc(gl_done, 1)
                    else:
                        cols_ = slice(int(g[1]) * G, (int(g[1]) + 1) * G)
                        dve.wait_ge(xr_in, 16)
                        dve.tensor_tensor(x2[:, c, cols_], chunk(g, c), xr[:, c, cols_], ALU.add).then_inc(saved_dve, 1)
                elif kind == "norm":
                    g, c = x
                    y = NORMS[x] - 1
                    n = GROUPS[g][1]
                    m, r, t = (z_[:, y % 2, 0:n] for z_ in (nm_, ny, nt_))
                    dve.wait_ge(ssum_done, y + 1)
                    dve.tensor_scalar(m, ps[:, 4 + y % 4, 0:n], 1.0 / (DH if g in "qk" else P), EPS, ALU.mult, ALU.add).then_inc(nm_ready, 1)
                    dve.wait_ge(nm_ready, y + 1)
                    dve.wait_ge(ny_ready, y + 1)
                    newton(r, m, t)
                    dve.wait_ge(saved_act, SAVED_ACT[x])
                    dve.scalar_tensor_tensor(normed_chunk(g, c), normed_chunk(g, c), GAIN[g], r, ALU.mult, ALU.mult).then_inc(normed, 1)
                elif kind == "msoft":
                    h, = x
                    dve.wait_ge(ms_done, h + 1)
                    link(dve.tensor_reduce(mmax, ps[:, 4:6, :].rearrange("p b (t m) -> p (b t) m", m=MEM), AX.X, ALU.max))
                    dve.tensor_scalar(mneg_, mmax, -SCALE_M, None, ALU.mult).then_inc(mneg_ready, 1)
                    dve.wait_ge(mexp_done, h + 1)
                    link(dve.reciprocal(mrec, msum))
                    for t in range(NT):
                        e_ = dve.tensor_scalar(pm[:, t, :], pm[:, t, :], mrec[:, t:t + 1], None, ALU.mult)
                    e_.then_inc(mprob_ready, 1)
                elif kind == "mturn":
                    h, = x
                    dve.wait_ge(mt_done, h + 1)
                    if h:
                        dve.wait_ge(mo_done, h)
                    dve.tensor_copy(pT[:, 1, :], ps[:, 7, :]).then_inc(mt_dve, 1)
                elif kind == "mout":
                    h, = x
                    dve.wait_ge(mo_done, h + 1)
                    dve.tensor_copy(om[:, h, :], ps[:, 4, :]).then_inc(om_saved, 1)
                elif kind == "soft":
                    h, = x
                    for n, b in enumerate(((2, 3), (0, 1))):
                        dve.wait_ge(log_done, 2 * h + n + 1)
                        for i in b:
                            e_ = dve.scalar_tensor_tensor(sp[:, OFF[i]:OFF[i] + WIDTH[i]], ps[:, 4 + i, P * i:SEQ], 0.0,
                                                          we[:, OFF[i]:OFF[i] + WIDTH[i]], ALU.max, ALU.add)
                        e_.then_inc(sp_done, 1)
                        dve.wait_ge(sp_done, 2 * h + n + 1)
                        lo, hi = OFF[b[0]], OFF[b[1]] + WIDTH[b[1]]
                        if h:
                            dve.wait_ge(c_done, NT * h)
                        dve.tensor_copy(sph[:, lo:hi], sp[:, lo:hi]).then_inc(sph_done, 1)
                        dve.wait_ge(sph_done, 2 * h + n + 1)
                        dve.tensor_tensor(spl[:, lo:hi], sp[:, lo:hi], sph[:, lo:hi].bitcast(F32), ALU.subtract).then_inc(spl_done, 1)
                elif kind == "av":
                    h, = x
                    lo = DH * (h % 2)
                    dve.wait_ge(av_done, h + 1)
                    dve.tensor_copy(osb[lo:lo + DH, h // 2, :], ps[lo:lo + DH, 4, :]).then_inc(o_saved, 1)
                elif kind == "osplit":
                    i, = x
                    dve.wait_ge(oh_done, i + 1)
                    dve.tensor_tensor(ol[i][:, :, :], (osb, oc, om)[i][:, :, :], oh[i][:, :, :].bitcast(F32), ALU.subtract).then_inc(osplit_done, 1)
            if not stop_after_mixer:
                routing_dve(dve, link, chain, newton)

        @block.gpsimd
        def _(pool):
            for r in range(NT + MT):
                src = a["mem"][0][(r - T0) * P:(r - T0 + 1) * P, :] if r >= T0 else a["x"][0][r * P:(r + 1) * P, :]
                pool.dma_start(xm[:, r, :], src).then_inc(xm_in[r], 16)
            count = [0]

            def after(ins):
                count[0] += 1
                ins.then_inc(made, 1)
                pool.wait_ge(made, count[0])

            for m, value in ((ident, 0.0), (identb, 0.0), (ones, 1.0), (onesb, 1.0), (halves, 0.0), (downf, -1.0),
                             (maskb, MASKED), (before, 1.0)):
                after(pool.memset(m[:, :], value))
            after(pool.memset(halves[0:DH, 0:DH], 1.0))
            after(pool.memset(halves[DH:P, DH:P], 1.0))
            for m, op, fill, step_, per in ((ident, ALU.not_equal, 1.0, -1, 1), (identb, ALU.not_equal, 1.0, -1, 1),
                                            (downf, ALU.is_ge, 0.0, -1, 1), (maskb, ALU.is_ge, 0.0, -1, 1),
                                            (before, ALU.is_gt, 0.0, 1, -1)):
                after(pool.affine_select(out=m[:, :], in_=m[:, :], compare_op=op, fill=fill, base=0, pattern=[[step_, P]],
                                         channel_multiplier=per))
            pool.wait_ge(unit_done, UNIT["g21", 1, 3])
            pool.dma_start(xr[:, :, :], a["x"][0].rearrange("(t p) d -> p t d", p=P)).then_inc(xr_in, 16)
            if stop_after_mixer:
                pool.wait_ge(saved_dve, SAVED_DVE["o1", NT - 1])
                pool.dma_start(out[0].rearrange("(t p) d -> p t d", p=P), x2[:, :, :]).then_inc(out_done, 16)
                pool.wait_ge(out_done, 16)
            else:
                routing_pool(pool)


_INS = ["x", "mem", "mix_norm_g", "w_in", "sb_q_norm_g", "sb_k_norm_g", "conv_w", "mem_norm_g", "w_mem_kv",
        "mem_q_norm_g", "mem_k_norm_g", "w_br_sb", "w_br_conv", "w_br_mem", "w_o", "ffn_norm_g", "w_router", "b_router",
        "w_gate_up", "b_gate_up", "w_down", "b_down"]
_OUTS = [((1, 512, 1024), "float32")]


def kernel(**inputs):
    import numpy as _np
    import concourse.bacc as _bacc
    from concourse import mybir as _mybir
    from concourse.bass_utils import run_bass_kernel_spmd as _run

    nc = _bacc.Bacc("TRN2", target_bir_lowering=False, num_devices=1)
    arrays, aps = {}, {}
    for name in _INS:
        x = _np.ascontiguousarray(inputs[name])
        arrays[f"in_{name}_dram"] = x
        aps[name] = nc.dram_tensor(f"in_{name}_dram", x.shape, _mybir.dt.from_np(x.dtype), kind="ExternalInput").ap()
    shape, dtype = _OUTS[0]
    out = nc.dram_tensor("out_0_dram", shape, _mybir.dt.from_np(_np.dtype(dtype)), kind="ExternalOutput").ap()
    build(nc, aps, out)
    r = _run(nc, [arrays], core_ids=[0])
    return r.results[0]["out_0_dram"]
```

```python
from contextlib import ExitStack

import concourse.bass as bass
from concourse import mybir

F32 = mybir.dt.float32
F32R = mybir.dt.float32r
BF16 = mybir.dt.bfloat16
U32 = mybir.dt.uint32
ALU = mybir.AluOpType
ACT = mybir.ActivationFunctionType
AX = mybir.AxisListType

P = 128
SEQ, D = 512, 1024
NT = SEQ // P
KD = D // P
MEM, MT = 256, 2
SBH, DH = 8, 64
MH = 4
G = 512
E, FF, TOPK = 32, 1024, 4
LIMIT, ALPHA, EPS = 7.0, 1.702, 1e-6
BLK = 128
NBLK = SEQ // BLK
COLS = NBLK * E
NEVER = 1 << 20
MASKED = -1e30

SLOTS = 6
BUFS = 4
SLOTS_MIX = 4
GU, DN = 8, 4

GROUPS = {"mk": (2, MEM, 4), "q": (2, SEQ, 4), "k": (2, SEQ, 4), "qm": (2, SEQ, 4), "mv": (2, G, MT), "v": (2, G, NT),
          "cc": (2, SEQ, 4), "cx": (2, SEQ, 4), "cb": (2, SEQ, 4)}
for _i in range(3):
    for _j in range(2):
        GROUPS[f"g{_i}{_j}"] = (2, SEQ, 4)
        GROUPS[f"b{_i}{_j}"] = (1, SEQ, 4)
for _j in range(2):
    GROUPS[f"o{_j}"] = (2, G, NT)
NORMED = ("mk", "q", "k", "qm")
TOKEN_MAJOR = ("mv", "v", "o0", "o1")
EARLY_GATES = ("g00", "g01", "g10")
W_IN_COLUMN = {"q": 0, "k": 1, "v": 2, "cb": 3, "cc": 4, "cx": 5, "qm": 6, "g00": 7, "g01": 8, "g10": 9, "g11": 10,
               "g20": 11, "g21": 12}


def plan_mixer():
    tiles, steps = [], []
    order = ["mk", "q", "k", "qm", "mv", "v", "cc", "cx", "cb", *EARLY_GATES, "b00", "b01", "b10", "g11", "b11",
             "g20", "b20", "g21", "b21", "o0", "o1"]
    for g in order:
        for t in range(GROUPS[g][0]):
            tiles.append((g, t))
    number = {x: n for n, x in enumerate(tiles)}

    def units(g):
        for t in range(GROUPS[g][0]):
            for c in range(GROUPS[g][2]):
                out = []
                if c == 0 and number[g, t] + 1 < len(tiles):
                    out.append(("split", number[g, t] + 1))
                out.append(("unit", g, t, c))
                if t == GROUPS[g][0] - 1:
                    out.append(("save", g, c))
                yield out

    steps += [("rms", "m"), ("turn", "m"), ("split", 0)]
    late = []
    for g in ("mk", "q", "k", "qm", "mv", "v"):
        for part in units(g):
            if part[-1] == ("unit", "mk", 0, 0):
                part.remove(("split", 1))
            if ("unit", "mk", 1, 0) in part:
                steps += [("rms", "x"), ("split", 1), ("turn", "x")]
            steps += part
            for x in late:
                steps.append(("ssum", *x))
                steps.append(("norm", *x))
            late = [part[-1][1:]] if part[-1][0] == "save" and g in NORMED else []
    beside = [part for g in ("cc", "cx", "cb") for part in units(g)]
    for h in range(MH):
        steps += [("mscore", h), ("msoft", h)]
        for _ in range(4):
            steps += beside.pop(0)
        steps += [("mturn", h)]
        for _ in range(2):
            steps += beside.pop(0)
        steps += [("mout", h)]
    beside = [part for g in EARLY_GATES for part in units(g)]
    for h in range(SBH):
        steps += [("z", h), ("soft", h)]
        if h and h % 2 == 0:
            steps += [("ochunk", h // 2 - 1)]
        for _ in range(2):
            steps += beside.pop(0)
        steps += [("between", h)]
        steps += beside.pop(0)
        steps += [("av", h)]
    assert not beside
    steps += [("ochunk", SBH // 2 - 1), ("sig", 0), ("osplit", 1), ("sig", 1), ("osplit", 2), ("sig", 2)]
    for g in order[order.index("b00"):]:
        for part in units(g):
            steps += part
            if any(x in part for x in (("unit", "o0", 1, 0), ("unit", "o1", 0, 0))):
                steps.append(("bias", sum(x[0] == "bias" for x in steps)))
            if part[-1][:2] == ("save", "o1"):
                c = part[-1][2]
                steps += {0: [("square", 0)], 1: [("square", 1)], 2: [("root", 0), ("square", 2)],
                          3: [("scale", 0), ("square", 3), ("root", 1), ("scale", 1)]}[c]
    return tiles, number, steps


TILES, NUMBER, STEPS = plan_mixer()
NM = len(TILES)


def ranks(keys):
    return {k: n + 1 for n, k in enumerate(keys)}


SAVES = [s[1:] for s in STEPS if s[0] == "save"]
BY_ACT = lambda g: g in (*NORMED, "mv", "v", "cc") or g[0] == "g"
SAVED_ACT = ranks(x for x in SAVES if BY_ACT(x[0]))
SAVED_DVE = ranks(x for x in SAVES if not BY_ACT(x[0]))
DONE_UNIT = ranks(SAVES)
NORMS = ranks(s[1:] for s in STEPS if s[0] == "norm")
BANK, FREED_BY = {}, {}
_last, _side = {}, 0
for _g in dict.fromkeys(x[0] for x in SAVES):
    _merge = _g[0] in "bo" or (_g[0] == "g" and _g not in EARLY_GATES)
    _side = 4 - _side if _merge else 0
    for _c in range(GROUPS[_g][2]):
        BANK[_g, _c] = _side + _c
        FREED_BY[_g, _c] = _last.get(_side + _c)
        _last[_side + _c] = (_g, _c)

WIDTH = [SEQ - P * i for i in range(NT)]
OFF = [sum(WIDTH[:i]) for i in range(NT)]
PACKED = sum(WIDTH)


def build(nc, a, out, stop_after_mixer=False):
    with ExitStack() as ctx:
        ctx.enter_context(nc.allow_non_contiguous_dma("small vectors laid along the partitions"))
        base = 16512

        def sb(name, shape, dt, kb):
            return nc.alloc_sbuf_tensor_at(name, shape, dt, offset=base + int(kb * 1024))

        def sem(name):
            return ctx.enter_context(nc.semaphore(name))

        ps = ctx.enter_context(nc.psum_tensor("ps", [P, 8, 512], F32))

        ring = sb("ring", [P, SLOTS, 2048], F32, 0)
        hh = sb("hh", [P, KD, SEQ], F32R, 32)
        hl = sb("hl", [P, KD, SEQ], F32R, 48)
        qT = sb("qT", [P, 4, SEQ], F32, 64)
        kT = sb("kT", [P, 4, SEQ], F32, 72)
        v = sb("v", [P, NT, G], F32, 80)
        cu = sb("cu", [P, 4, SEQ], F32, 88)
        we = sb("we", [P, PACKED], F32, 88)
        oh = [sb("o0h", [P, 4, SEQ], F32R, 64), sb("o1h", [P, 4, SEQ], F32R, 80), sb("o2h", [P, 4, SEQ], F32R, 186)]
        ol = [sb("o0l", [P, 4, SEQ], F32R, 72), sb("o1l", [P, 4, SEQ], F32R, 88), sb("o2l", [P, 4, SEQ], F32R, 194)]
        gh = sb("gh", [P, KD, SEQ], F32R, 64)
        gl = sb("gl", [P, KD, SEQ], F32R, 80)
        xr = sb("xr", [P, NT, D], F32, 32)
        x2 = sb("x2", [P, NT, D], F32, 48)
        wh = sb("wh", [P, 2, 2048], F32R, 96)
        wl = sb("wl", [P, 2, 2048], F32R, 112)
        ident = sb("ident", [P, P], F32, 128)
        ones = sb("ones", [P, P], F32, 128.5)
        halves = sb("halves", [P, P], F32, 129)
        down = sb("down", [P, P], F32R, 129.5)
        minus = sb("minus", [P, P], F32R, 130)
        identb = sb("identb", [P, P], BF16, 130.5)
        maskb = sb("maskb", [P, P], BF16, 130.75)
        before = sb("before", [P, P], BF16, 131)
        onesb = sb("onesb", [P, P], BF16, 131.25)
        downf = sb("downf", [P, P], F32, 131.5)
        gbc = sb("gbc", [P, D], F32, 132)
        small = sb("small", [P, 384], F32, 136)
        xm = sb("xm", [P, NT + MT, D], F32, 138)
        mh = sb("mh", [P, KD, MEM], F32R, 162)
        ml = sb("ml", [P, KD, MEM], F32R, 170)
        sqd = sb("sqd", [P, D], F32, 186)
        km = sb("km", [P, MH, MEM], F32, 138)
        vm = sb("vm", [P, MT, G], F32, 142)
        osb = sb("osb", [P, 4, SEQ], F32, 138)
        om = sb("om", [P, 4, SEQ], F32, 146)
        oc = sb("oc", [P, 4, SEQ], F32, 154)
        qm = sb("qm", [P, MH, SEQ], F32, 178)
        gate = sb("gate", [P, 3, 4, SEQ], F32, 162)
        nsq = sb("nsq", [P, 2, SEQ], F32, 186)
        nm_ = sb("nm_", [P, 2, SEQ], F32, 190)
        ny = sb("ny", [P, 2, SEQ], F32, 194)
        nt_ = sb("nt_", [P, 2, SEQ], F32, 198)
        pm = sb("pm", [P, NT, MEM], F32, 186)
        pT = sb("pT", [P, MT, SEQ], F32, 190)
        sp = sb("sp", [P, PACKED], F32, 186)
        sph = sb("sph", [P, PACKED], F32R, 191)
        spl = sb("spl", [P, PACKED], F32R, 196)
        w = sb("w", [P, PACKED], F32, 201)

        acc = sb("acc", [P, KD, SEQ], F32, 138)
        tmp = sb("tmp", [P, 2, SEQ], F32, 202)
        sq2 = sb("sq2", [P, D], F32, 138)
        hf = sb("hf", [P, NT, D], F32, 154)
        hfT = sb("hfT", [P, KD, SEQ], F32, 170)
        rt = sb("rt", [P, 1740], F32, 186)
        eh = sb("eh", [P, BUFS, 2048], F32R, 64)
        el = sb("el", [P, BUFS, 2048], F32R, 96)
        ebias = sb("ebias", [3 * E, 3 * FF], BF16, 198)
        braw = sb("braw", [3 * E, 3 * FF], F32, 170)
        pick = sb("pick", [3 * E, E * P], BF16, 146)
        xg = sb("xg", [P, D], F32, 142)
        xh = sb("xh", [P, KD, P], F32R, 158)
        xl = sb("xl", [P, KD, P], F32R, 162)
        gm = sb("gm", [P, FF], F32, 166)
        lc = sb("lc", [P, FF], F32, 170)
        sg = sb("sg", [P, FF], F32, 174)
        ac = sb("ac", [P, FF], F32, 178)
        ah = sb("ah", [P, KD, P], F32R, 182)
        al = sb("al", [P, KD, P], F32R, 186)
        yo = sb("yo", [P, D], F32, 190)
        tok = sb("tok", [P, COLS], U32, 204)
        row = sb("row", [P, COLS], U32, 205)
        gw = sb("gw", [P, NT, TOPK], F32, 206.25)
        now = sb("now", [P, 4], U32, 206.5)
        most = sb("most", [P, 4], U32, 206.625)
        wide = sb("wide", [P, GU, 2048], F32, 64)
        xf = sb("xf", [P, KD, P], F32, 158)
        af = sb("af", [P, KD, P], F32, 182)
        yg = sb("yg", [P, NT, TOPK, D], F32, 64)

        def cols(a0, n):
            return small[:, a0:a0 + n]
        mixg, memg = cols(0, KD), cols(8, KD)
        qg, kg, qmg, kmg = cols(16, 1), cols(17, 1), cols(18, 1), cols(19, 1)
        taps = cols(20, 12)
        ssx, mx_, rx, tx = cols(32, 6), cols(38, 6), cols(44, 6), cols(50, 6)
        mmax, mneg_, msum, mrec = cols(56, 4), cols(60, 4), cols(64, 4), cols(68, 4)
        ss2, m2, r2, t2 = cols(72, 4), cols(76, 4), cols(80, 4), cols(84, 4)
        gneg, gsum, grec = cols(88, 4), cols(92, 4), cols(120, 4)
        bro = small[0:1, 328:360]
        wr = sb("wr", [P, KD, E], F32, 194)

        def rcols(a0, n, m=None):
            x = rt[:, a0:a0 + n]
            return x if m is None else x.rearrange("p (a b) -> p a b", b=m)
        lg = rcols(0, 128, E)
        v8 = rcols(128, 32, 8)
        i8f = rcols(160, 32, 8)
        oneh = rcols(192, 512, E)
        msk = rcols(704, 128, E)
        posf = rcols(832, 128, E)
        junk = rcols(960, 128)
        pk, jj, tif = rcols(1088, 16), rcols(1120, 16), rcols(1136, 16)
        iotaf = rcols(1152, COLS)
        rowf = rcols(1152 + COLS, NT * TOPK)
        i8 = sb("i8", [P, NT, 8], U32, 193)
        rows = sb("rows", [P, NT * TOPK], U32, 193.375)
        lgT = sb("lgT", [E, SEQ], F32, 138)
        emptyf = oneh.rearrange("p x e -> p (x e)")[:, 0:COLS]
        slot_is = sb("slot_is", [P, NT * TOPK, P], F32, 154)
        row_at = sb("row_at", [P, NT * TOPK, COLS], F32, 162)
        mskb = sb("mskb", [P, NT, E], BF16, 193.5)
        iotai = sb("iotai", [P, COLS], U32, 142)

        hf_d = nc.dram_tensor("hf_scratch", (SEQ, D), F32).ap()
        y_d = nc.dram_tensor("y_scratch", (SEQ * TOPK, D), F32).ap()

        gain_in, small_in = sem("gain_in"), sem("small_in")
        xm_in = [sem(f"xm_in{r}") for r in range(NT + MT)]
        w_in = [sem(f"w_in{s}") for s in range(SLOTS)]
        made = sem("made")
        made_dve = sem("made_dve")
        squared = sem("squared")
        mean_ready, root_ready, scaled = sem("mean_ready"), sem("root_ready"), sem("scaled")
        turned, h_hi, h_lo = sem("turned"), sem("h_hi"), sem("h_lo")
        w_hi, w_lo = sem("w_hi"), sem("w_lo")
        unit_done, saved_act, saved_dve = sem("unit_done"), sem("saved_act"), sem("saved_dve")
        nsq_ready, ssum_done, nm_ready, ny_ready, normed = (sem(x) for x in ("nsq_ready", "ssum_done", "nm_ready", "ny_ready", "normed"))
        ms_done, mneg_ready, mexp_done, mprob_ready, mt_done, mt_act, mt_dve, mo_done, om_saved = (
            sem(x) for x in ("ms_done", "mneg_ready", "mexp_done", "mprob_ready", "mt_done", "mt_act", "mt_dve", "mo_done", "om_saved"))
        z_done, log_done, sp_done, sph_done, spl_done, c_done, w_done, av_done, o_saved = (
            sem(x) for x in ("z_done", "log_done", "sp_done", "sph_done", "spl_done", "c_done", "w_done", "av_done", "o_saved"))
        oh_done, osplit_done, sig_done, acc_done, gh_done, gl_done = (
            sem(x) for x in ("oh_done", "osplit_done", "sig_done", "acc_done", "gh_done", "gl_done"))
        xr_in, squared2, m2_ready, r2_ready, hf_done, hf_turned, hfT_act, logitT_done, lgT_ready, logit_done = (
            sem(x) for x in ("xr_in", "squared2", "m2_ready", "r2_ready", "hf_done", "hf_turned", "hfT_act", "logitT_done", "lgT_ready", "logit_done"))
        hf_out = sem("hf_out")
        act_step, dve_step, pool_step = sem("act_step"), sem("dve_step"), sem("pool_step")
        out_done = sem("out_done")

        def operands(g):
            if g[0] == "m":
                return mh, ml
            if g[0] == "b":
                return oh[int(g[1])], ol[int(g[1])]
            return (gh, gl) if g[0] == "o" else (hh, hl)

        def weight_source(g, t):
            lo, hi = t * 4 * P, (t + 1) * 4 * P
            if g in W_IN_COLUMN:
                src, c = a["w_in"][0], W_IN_COLUMN[g] * G
            elif g in ("mk", "mv"):
                src, c = a["w_mem_kv"][0], G * (g == "mv")
            elif g[0] == "b":
                src, c = a[("w_br_sb", "w_br_conv", "w_br_mem")[int(g[1])]][0], int(g[2]) * G
            else:
                src, c = a["w_o"][0], int(g[1]) * G
            return src[lo:hi, c:c + G].rearrange("(k p) n -> p k n", p=P)

        UNIT = ranks(s[1:] for s in STEPS if s[0] == "unit")
        USED = {n: UNIT[g, t, GROUPS[g][2] - 1] for n, (g, t) in enumerate(TILES)}
        SUMMED = {(g, c): UNIT[g, GROUPS[g][0] - 1, c] for g, c in SAVES}
        LATE = {"g11": (0, "b00"), "g20": (1, "b01"), "g21": (2, "b10")}
        PLACE = {"b00": 0, "b01": 1, "b10": 2, "b11": 0, "b20": 1, "b21": 2}
        TILES_OF = {"m": range(NT, NT + MT), "x": range(NT)}
        BEFORE = {"m": 0, "x": MT}
        HALF = {"m": (memg, mh, ml, MEM), "x": (mixg, hh, hl, SEQ)}

        def turn_bank(which, k):
            return k if which == "m" else 4 + k % 4

        def split(n):
            return wh[:, n % 2, :], wl[:, n % 2, :]

        def chunk(g, c):
            n = GROUPS[g][1]
            return ps[:, BANK[g, c], 0:n]

        def normed_chunk(g, c):
            return {"mk": km, "q": qT, "k": kT, "qm": qm}[g][:, c, :]

        GAIN = {"mk": kmg, "q": qg, "k": kg, "qm": qmg}
        SCALE_M = float(P) ** -0.5

        MADE = 15
        first_loads = [(memg, a["mem_norm_g"][0].rearrange("(k p) -> p k", p=P)), (mixg, a["mix_norm_g"][0].rearrange("(k p) -> p k", p=P))]
        small_loads = [(qmg, a["mem_q_norm_g"][0].rearrange("(p o) -> p o", o=1)), (kmg, a["mem_k_norm_g"][0].rearrange("(p o) -> p o", o=1)),
                       (bro, a["b_router"]), (gbc[:, :], a["ffn_norm_g"].broadcast_to([P, D]))]
        for half in range(2):
            for dst, name in ((qg, "sb_q_norm_g"), (kg, "sb_k_norm_g")):
                small_loads.append((dst[half * DH:(half + 1) * DH, :], a[name][0].rearrange("(p o) -> p o", o=1)))
        for j in range(3):
            small_loads.append((taps[:, 4 * j:4 * j + 4], a["conv_w"][0][j].rearrange("(c p) -> p c", p=P)))


        choice_ready, slots_done, tok_ready, most_ready = (sem(x) for x in ("choice_ready", "slots_done", "tok_ready", "most_ready"))
        wr_in, rmade, best_ready, gexp_done, msk_ready, pos_done, braw_in, ebias_ready, picks_ready, iota_read = (
            sem(x) for x in ("wr_in", "rmade", "best_ready", "gexp_done", "msk_ready", "pos_done", "braw_in", "ebias_ready", "picks_ready", "iota_read"))
        e_used = sem("e_used")
        xg_in, x_turned, xh_done, x_split = (sem(x) for x in ("xg_in", "x_turned", "xh_done", "x_split"))
        lin_done, pool_now = sem("lin_done"), sem("pool_now")
        gu_free, gm_done, sg_done, ac_done, a_turned, ah_done, a_split = (
            sem(x) for x in ("gu_free", "gm_done", "sg_done", "ac_done", "a_turned", "ah_done", "a_split"))
        dn_free, y_out = sem("dn_free"), sem("y_out")
        more_x, more_xf, more_gu, more_act, more_lin, more_af, more_dn, more_y, more_sig, more_w, more_turn = (
            sem(x) for x in ("more_x", "more_xf", "more_gu", "more_act", "more_lin", "more_af", "more_dn", "more_y", "more_sig",
                             "more_w", "more_turn"))
        yg_in = [sem(f"yg_in{x_}") for x_ in range(NT * TOPK)]
        summed = sem("summed")

        SIDE = BANK["o0", 0]
        LOGIT = BANK["o1", 0]
        SLOT = SIDE + 1
        ROUTE = SIDE
        USES = NM // SLOTS_MIX
        assert NM % SLOTS_MIX == 0 and NM % 2 == 0
        PER = GU + DN
        EARLY = NT - 1

        def at(e, n):
            return NM + n if isinstance(e, int) and e == 0 else e * PER + (NM - DN + n)

        def gate_up(e, k):
            return a["w_gate_up"][0][e, k * P:(k + 1) * P, :]

        def down_tile(e, m):
            return a["w_down"][0][e, m * 2 * P:(m + 1) * 2 * P, :].rearrange("(k p) n -> p k n", p=P)

        def landed(eng, e, n):
            s, again = n % SLOTS, n // SLOTS
            before_it = USES if s < SLOTS_MIX else 0
            if isinstance(e, int) and e == 0:
                eng.wait_ge(w_in[s], 16 * (before_it + again + 1))
            else:
                first = 2 if s + SLOTS < GU else 1
                eng.wait_ge(w_in[s], e * (16 * PER // SLOTS) + 16 * (before_it + first - PER // SLOTS + again + 1))

        def iterations(eng, body):
            for e in range(3):
                body(e)
            with eng.Fori(3, E) as e:
                body(e)
            body(None)

        def experts_sync(sp_):
            def load(e, n):
                if isinstance(e, int) and e == 0:
                    if n >= SLOTS:
                        sp_.wait_ge(w_lo, at(0, n - SLOTS) + 1)
                    elif n < SLOTS_MIX:
                        sp_.wait_ge(w_lo, NM - SLOTS_MIX + n + 1)
                    else:
                        sp_.wait_ge(saved_dve, SAVED_DVE["o1", NT - 1])
                elif n >= SLOTS:
                    sp_.wait_ge(w_lo, at(e, n - SLOTS) + 1)
                elif isinstance(e, int) and e == 1:
                    sp_.wait_ge(w_lo, at(0, n + SLOTS if n + SLOTS < GU else n) + 1)
                else:
                    sp_.wait_ge(w_lo, at(e - 1, n + SLOTS) + 1)
                slot = ring[:, n % SLOTS, :]
                if n < GU:
                    sp_.dma_start(slot, gate_up(e, n)).then_inc(w_in[n % SLOTS], 16)
                else:
                    sp_.dma_start(slot.rearrange("p (k n) -> p k n", k=2), down_tile(e - 1, n - GU)).then_inc(w_in[n % SLOTS], 16)

            def body(e):
                if e is None:
                    for m in range(DN):
                        sp_.wait_ge(w_lo, at(E - 1, m + SLOTS) + 1)
                        sp_.dma_start(ring[:, m, :].rearrange("p (k n) -> p k n", k=2), down_tile(E - 1, m)).then_inc(w_in[m], 16)
                    return
                for n in range(GU if isinstance(e, int) and e == 0 else PER):
                    load(e, n)

            iterations(sp_, body)
            sp_.wait_ge(most_ready, 1)
            sp_.wait_ge(y_out, 16 * E)
            many = sp_.value_load(most[0:1, 0:1], min_val=0, max_val=SEQ)
            with sp_.If(many > BLK):
                with sp_.Fori(1, NBLK) as j:
                    with sp_.Fori(0, E) as e:
                        sp_.wait_ge(y_out, (j * E + e) * 16)
                        for k in range(GU):
                            sp_.dma_start(wide[:, k, :], gate_up(e, k)).then_inc(more_w, 16)
                        for m in range(DN):
                            sp_.dma_start(ring[:, m, :].rearrange("p (k n) -> p k n", k=2), down_tile(e, m)).then_inc(more_w, 16)
                sp_.wait_ge(y_out, 16 * E * NBLK)
            for t in range(NT):
                for k in range(TOPK):
                    sp_.dma_start(yg[:, t, k, :], y_d.rearrange("(t p k) d -> t k p d", p=P, k=TOPK)[t, k]).then_inc(yg_in[t * TOPK + k], 16)
            for t in range(NT):
                sp_.wait_ge(summed, 1 + t)
                sp_.dma_start(out[0][t * P:(t + 1) * P, :], x2[:, t, :]).then_inc(out_done, 16)
            sp_.wait_ge(out_done, 16 * NT)

        def routing_act(act):
            def hi_split(e, n):
                landed(act, e, n)
                if isinstance(e, int) and e == 0:
                    if n == 0:
                        act.wait_ge(unit_done, USED[NM - 1])
                    if n >= BUFS:
                        act.wait_ge(e_used, n - BUFS + 1)
                else:
                    act.wait_ge(e_used, e * PER + (n + 1 - DN - BUFS))
                act.activation(eh[:, n % BUFS, :], ring[:, n % SLOTS, :], ACT.Copy).then_inc(w_hi, 1)

            def save_logits(t):
                act.wait_ge(logitT_done, t + 1)
                act.activation(lgT[:, t * P:(t + 1) * P], ps[0:E, LOGIT + t, 0:P], ACT.Copy).then_inc(lgT_ready, 1)

            act.wait_ge(ebias_ready, 3)
            for t in range(NT):
                act.wait_ge(hf_done, t + 1)
                act.dma_start(hf_d[t * P:(t + 1) * P, :], hf[:, t, :]).then_inc(hf_out, 16)
                act.wait_ge(hf_turned, t + 1)
                for z_ in range(2):
                    i_ = act.activation(hfT[:, 4 * z_:4 * z_ + 4, t * P:(t + 1) * P],
                                        ps[:, SIDE + 2 * (t % 2) + z_, :].rearrange("p (k n) -> p k n", k=4), ACT.Copy)
                i_.then_inc(hfT_act, 1)
                if t:
                    save_logits(t - 1)
                    hi_split(0, t - 1)
            save_logits(NT - 1)
            act.wait_ge(best_ready, 1)
            for t in range(NT):
                i_ = act.activation(gw[:, t, :], v8[:, t, 0:TOPK], ACT.Exp, bias=gneg[:, t:t + 1], accum_out=gsum[:, t:t + 1])
            i_.then_inc(gexp_done, 1)

            def x_hi(e):
                act.wait_ge(x_turned, e + 1)
                for z_ in range(2):
                    i_ = act.activation(xh[:, 4 * z_:4 * z_ + 4, :], ps[:, 6 + z_, :].rearrange("p (k n) -> p k n", k=4), ACT.Copy)
                i_.then_inc(xh_done, 1)

            def a_hi(e):
                act.wait_ge(a_turned, e + 1)
                for z_ in range(2):
                    i_ = act.activation(ah[:, 4 * z_:4 * z_ + 4, :], ps[:, 6 + z_, :].rearrange("p (k n) -> p k n", k=4), ACT.Copy)
                i_.then_inc(ah_done, 1)

            def sig(e):
                act.wait_ge(gm_done, e + 1)
                act.activation(sg[:, :], gm[:, :], ACT.Sigmoid, scale=ALPHA).then_inc(sg_done, 1)

            def save_y(e, used):
                act.wait_ge(e_used, used)
                if not (isinstance(e, int) and e == 0):
                    act.wait_ge(y_out, e * 16)
                for z_ in range(2):
                    i_ = act.activation(yo[:, 512 * z_:512 * z_ + 512], ps[:, 4 + z_, :], ACT.Copy)
                i_.then_inc(dn_free, 1)

            def body(e):
                if e is None:
                    for m in range(DN):
                        hi_split(E, m)
                        if m == 1:
                            a_hi(E - 1)
                            save_y(E - 2, E * PER - DN)
                    save_y(E - 1, E * PER)
                    return
                first = isinstance(e, int) and e == 0
                for n in range(EARLY if first else 0, GU if first else PER):
                    hi_split(e, n)
                    if n == 1 and not (isinstance(e, int) and e < 2):
                        save_y(e - 2, e * PER - DN)
                    if n == BUFS - 1:
                        x_hi(0) if first else a_hi(e - 1)
                x_hi(e + 1)
                sig(e)

            iterations(act, body)
            act.wait_ge(y_out, 16 * E)
            act.wait_ge(most_ready, 1)
            many = act.value_load(most[0:1, 0:1], min_val=0, max_val=SEQ)
            with act.If(many > BLK):
                with act.Fori(1, E * (NBLK - 1) + 1) as b:
                    act.wait_ge(more_turn, 2 * b - 1)
                    for z_ in range(2):
                        i_ = act.activation(xf[:, 4 * z_:4 * z_ + 4, :], ps[:, 6 + z_, :].rearrange("p (k n) -> p k n", k=4), ACT.Copy)
                    i_.then_inc(more_xf, 1)
                    act.wait_ge(more_act, 2 * b - 1)
                    act.activation(sg[:, :], gm[:, :], ACT.Sigmoid, scale=ALPHA).then_inc(more_sig, 1)
                    act.wait_ge(more_turn, 2 * b)
                    for z_ in range(2):
                        i_ = act.activation(af[:, 4 * z_:4 * z_ + 4, :], ps[:, 6 + z_, :].rearrange("p (k n) -> p k n", k=4), ACT.Copy)
                    i_.then_inc(more_af, 1)
                    act.wait_ge(more_dn, b)
                    for z_ in range(2):
                        i_ = act.activation(yo[:, 512 * z_:512 * z_ + 512], ps[:, 4 + z_, :], ACT.Copy)
                    i_.then_inc(more_y, 1)

        def routing_pe(pe):
            def turn_hf(t):
                pe.wait_ge(hf_done, t + 1)
                if t == 0:
                    pe.wait_ge(saved_dve, SAVED_DVE["o1", NT - 1])
                for k in range(KD):
                    mm = pe.transpose(ps[:, SIDE + 2 * (t % 2) + k // 4, (k % 4) * P:(k % 4 + 1) * P], hf[:, t, k * P:(k + 1) * P], ident[:, :])
                mm.then_inc(hf_turned, 1)

            def turn_logits(t):
                pe.wait_ge(lgT_ready, t + 1)
                pe.transpose(ps[:, LOGIT + t, P:P + E], lgT[:, t * P:(t + 1) * P], ident[0:E, 0:E]).then_inc(logit_done, 1)

            turn_hf(0)
            turn_hf(1)
            pe.wait_ge(wr_in, 16)
            for t in range(NT):
                pe.wait_ge(hfT_act, t + 1)
                for k in range(KD):
                    pe.matmul(ps[0:E, LOGIT + t, 0:P], wr[:, k, :], hfT[:, k, t * P:(t + 1) * P], start=(k == 0), stop=False)
                pe.matmul(ps[0:E, LOGIT + t, 0:P], bro, ones[0:1, :], start=False, stop=True).then_inc(logitT_done, 1)
                if t + 2 < NT:
                    turn_hf(t + 2)
                if t:
                    turn_logits(t - 1)
            turn_logits(NT - 1)
            pe.wait_ge(msk_ready, 1)
            for t in range(NT):
                for u in range(t + 1):
                    pe.matmul(ps[:, ROUTE, t * E:(t + 1) * E], (before if u == t else onesb)[:, :], mskb[:, u, :],
                              start=(u == 0), stop=(u == t))
            for u in range(NT):
                mm = pe.matmul(ps[:, ROUTE, NT * E:(NT + 1) * E], onesb[:, :], mskb[:, u, :], start=(u == 0), stop=(u == NT - 1))
            mm.then_inc(pos_done, 1)

            for x_ in range(NT * TOPK):
                pe.wait_ge(choice_ready, x_ + 1)
                mm = pe.matmul(ps[:, SLOT, 0:COLS], slot_is[:, x_, :], row_at[:, x_, :], start=(x_ == 0), stop=(x_ == NT * TOPK - 1))
            mm.then_inc(slots_done, 1)

            def turn_x(e):
                pe.wait_ge(xg_in, (e + 1) * 16)
                if not (isinstance(e, int) and e <= 1):
                    pe.wait_ge(a_split, e - 1)
                for k in range(KD):
                    mm = pe.transpose(ps[:, 6 + k // 4, (k % 4) * P:(k % 4 + 1) * P], xg[:, k * P:(k + 1) * P], ident[:, :])
                mm.then_inc(x_turned, 1)

            def turn_a(e):
                pe.wait_ge(ac_done, e + 1)
                pe.wait_ge(x_split, e + 2)
                for k in range(KD):
                    mm = pe.transpose(ps[:, 6 + k // 4, (k % 4) * P:(k % 4 + 1) * P], ac[:, k * P:(k + 1) * P], ident[:, :])
                mm.then_inc(a_turned, 1)

            def run_gu(e):
                if not (isinstance(e, int) and e == 0):
                    pe.wait_ge(gu_free, e * 2)
                for n in range(4):
                    pe.matmul(ps[:, n, :], pick[:, bass.ds(e * P, P)], ebias[:, 512 * n:512 * n + 512], start=True, stop=False)
                pe.wait_ge(x_split, e + 1)
                for k in range(GU):
                    pe.wait_ge(w_lo, at(e, k) + 1)
                    for z_, (x_, w_) in enumerate(((xh, eh), (xh, el), (xl, eh))):
                        for n in range(4):
                            mm = pe.matmul(ps[:, n, :], x_[:, k, :], w_[:, k % BUFS, 512 * n:512 * n + 512], start=False,
                                           stop=(k == GU - 1 and z_ == 2))
                    mm.then_inc(e_used, 1)

            def run_dn(e, i, first):
                if not (isinstance(e, int) and e == 0):
                    pe.wait_ge(dn_free, e)
                for n in range(2):
                    pe.matmul(ps[:, 4 + n, :], pick[:, bass.ds(e * P, P)], ebias[:, 2 * FF + 512 * n:2 * FF + 512 * n + 512], start=True, stop=False)
                pe.wait_ge(a_split, e + 1)
                for m in range(DN):
                    pe.wait_ge(w_lo, at(i, first + m) + 1)
                    for kk in range(2):
                        for z_, (x_, w_) in enumerate(((ah, eh), (ah, el), (al, eh))):
                            for n in range(2):
                                mm = pe.matmul(ps[:, 4 + n, :], x_[:, 2 * m + kk, :],
                                               w_[:, m % BUFS, FF * kk + 512 * n:FF * kk + 512 * n + 512], start=False,
                                               stop=(m == DN - 1 and kk == 1 and z_ == 2))
                    mm.then_inc(e_used, 1)

            def body(e):
                if e is None:
                    run_dn(E - 1, E, 0)
                    return
                run_gu(e)
                turn_x(e + 1)
                if not (isinstance(e, int) and e == 0):
                    run_dn(e - 1, e, GU)
                turn_a(e)

            pe.wait_ge(most_ready, 1)
            turn_x(0)
            pe.wait_ge(picks_ready, 1)
            pe.wait_ge(ebias_ready, 3)
            iterations(pe, body)
            pe.wait_ge(y_out, 16 * E)
            many = pe.value_load(most[0:1, 0:1], min_val=0, max_val=SEQ)
            with pe.If(many > BLK):
                with pe.Fori(1, NBLK) as j:
                    with pe.Fori(0, E) as e:
                        b = j * E + e - (E - 1)
                        pe.wait_ge(more_x, b * 16)
                        for k in range(KD):
                            mm = pe.transpose(ps[:, 6 + k // 4, (k % 4) * P:(k % 4 + 1) * P], xg[:, k * P:(k + 1) * P], ident[:, :])
                        mm.then_inc(more_turn, 1)
                        for n in range(4):
                            pe.matmul(ps[:, n, :], pick[:, bass.ds(e * P, P)], ebias[:, 512 * n:512 * n + 512], start=True, stop=False)
                        pe.wait_ge(more_xf, b)
                        pe.wait_ge(more_w, b * PER * 16)
                        for k in range(GU):
                            for n in range(4):
                                mm = pe.matmul(ps[:, n, :], xf[:, k, :], wide[:, k, 512 * n:512 * n + 512], start=False, stop=(k == GU - 1))
                        mm.then_inc(more_gu, 1)
                        pe.wait_ge(more_act, 2 * b)
                        for k in range(KD):
                            mm = pe.transpose(ps[:, 6 + k // 4, (k % 4) * P:(k % 4 + 1) * P], ac[:, k * P:(k + 1) * P], ident[:, :])
                        mm.then_inc(more_turn, 1)
                        for n in range(2):
                            pe.matmul(ps[:, 4 + n, :], pick[:, bass.ds(e * P, P)], ebias[:, 2 * FF + 512 * n:2 * FF + 512 * n + 512], start=True, stop=False)
                        pe.wait_ge(more_af, b)
                        for k in range(KD):
                            for n in range(2):
                                mm = pe.matmul(ps[:, 4 + n, :], af[:, k, :], ring[:, k // 2, FF * (k % 2) + 512 * n:FF * (k % 2) + 512 * n + 512],
                                               start=False, stop=(k == KD - 1))
                        mm.then_inc(more_dn, 1)

        def routing_dve(dve, link):
            def lo_split(e, n):
                dve.wait_ge(w_hi, at(e, n) + 1)
                dve.tensor_tensor(el[:, n % BUFS, :], ring[:, n % SLOTS, :], eh[:, n % BUFS, :].bitcast(F32), ALU.subtract).then_inc(w_lo, 1)

            dve.wait_ge(rmade, 1)
            dve.tensor_copy(iotaf, iotai[:, :]).then_inc(iota_read, 1)
            link(dve.tensor_scalar(rowf, rows[:, :], 1.0, None, ALU.add))
            for t in range(NT):
                if t < EARLY:
                    lo_split(0, t)
                dve.wait_ge(logit_done, t + 1)
                link(dve.tensor_copy(lg[:, t, :], ps[:, LOGIT + t, P:P + E]))
                link(dve.max(v8[:, t, :], lg[:, t, :]))
                link(dve.max_index(i8[:, t, :], v8[:, t, :], lg[:, t, :]))
                link(dve.tensor_copy(i8f[:, t, :], i8[:, t, :]))
                for k in range(TOPK):
                    i_ = dve.tensor_scalar(oneh[:, t * TOPK + k, :], iotaf[:, 0:E], i8f[:, t, k:k + 1], None, ALU.is_equal)
            link(i_)
            by_k = oneh.rearrange("p (t k) e -> p k t e", k=TOPK)
            link(dve.tensor_tensor(msk, by_k[:, 0], by_k[:, 1], ALU.add))
            link(dve.tensor_tensor(msk, msk, by_k[:, 2], ALU.add))
            dve.tensor_tensor(mskb[:, :, :], msk, by_k[:, 3], ALU.add).then_inc(msk_ready, 1)
            dve.tensor_scalar(gneg, v8[:, :, 0], -1.0, None, ALU.mult).then_inc(best_ready, 1)
            dve.wait_ge(pos_done, 1)
            link(dve.tensor_copy(posf, ps[:, ROUTE, 0:NT * E].rearrange("p (t e) -> p t e", e=E)))
            for k in range(TOPK):
                i_ = dve.tensor_tensor(by_k[:, k], by_k[:, k], posf, ALU.mult)
            link(i_)
            link(dve.tensor_reduce(pk, oneh, AX.X, ALU.add))
            link(dve.tensor_scalar(jj, pk, float(BLK), None, ALU.is_ge))
            for b in range(2, NBLK):
                link(dve.tensor_scalar(tif, pk, float(BLK * b), None, ALU.is_ge))
                link(dve.tensor_tensor(jj, jj, tif, ALU.add))
            dve.scalar_tensor_tensor(pk, jj, float(-BLK), pk, ALU.mult, ALU.add)
            link(dve.scalar_tensor_tensor(tif.rearrange("p (t k) -> p t k", k=TOPK), jj.rearrange("p (t k) -> p t k", k=TOPK), float(E),
                                          i8f[:, :, 0:TOPK], ALU.mult, ALU.add))
            dve.wait_ge(hf_out, 16 * NT)
            dve.wait_ge(logit_done, NT)
            for x_ in range(NT * TOPK):
                dve.tensor_scalar(slot_is[:, x_, :], iotaf[:, 0:P], pk[:, x_:x_ + 1], None, ALU.is_equal)
                dve.tensor_scalar(row_at[:, x_, :], iotaf, tif[:, x_:x_ + 1], rowf[:, x_:x_ + 1], ALU.is_equal, ALU.mult).then_inc(choice_ready, 1)
            dve.wait_ge(slots_done, 1)
            link(dve.tensor_scalar(emptyf, ps[:, SLOT, 0:COLS], 0.5, float(NEVER), ALU.is_lt, ALU.mult))
            link(dve.scalar_tensor_tensor(row[:, :], ps[:, SLOT, 0:COLS], -1.0, emptyf, ALU.add, ALU.add))
            dve.tensor_scalar(tok[:, :], row[:, :], TOPK.bit_length() - 1, None, ALU.logical_shift_right).then_inc(tok_ready, 1)
            link(dve.tensor_reduce(junk[:, 0:1], ps[:, ROUTE, NT * E:(NT + 1) * E], AX.X, ALU.max))
            dve.tensor_copy(most[:, 0:1], junk[:, 0:1]).then_inc(most_ready, 1)
            dve.wait_ge(gexp_done, 1)
            link(dve.reciprocal(grec, gsum))
            for t in range(NT):
                i_ = dve.tensor_scalar(gw[:, t, :], gw[:, t, :], grec[:, t:t + 1], None, ALU.mult)
            link(i_)
            def x_lo(e):
                dve.wait_ge(xh_done, e + 1)
                for z_ in range(2):
                    i_ = dve.tensor_tensor(xl[:, 4 * z_:4 * z_ + 4, :], ps[:, 6 + z_, :].rearrange("p (k n) -> p k n", k=4),
                                           xh[:, 4 * z_:4 * z_ + 4, :].bitcast(F32), ALU.subtract)
                i_.then_inc(x_split, 1)

            def a_lo(e):
                dve.wait_ge(ah_done, e + 1)
                for z_ in range(2):
                    i_ = dve.tensor_tensor(al[:, 4 * z_:4 * z_ + 4, :], ps[:, 6 + z_, :].rearrange("p (k n) -> p k n", k=4),
                                           ah[:, 4 * z_:4 * z_ + 4, :].bitcast(F32), ALU.subtract)
                i_.then_inc(a_split, 1)

            def clamp_gate(e):
                dve.wait_ge(e_used, e * PER + (GU - DN) if not (isinstance(e, int) and e == 0) else GU)
                dve.tensor_scalar(gm[:, :].rearrange("p (b n) -> p b n", b=2), ps[:, 0:2, :], LIMIT, None, ALU.min).then_inc(gm_done, 1)

            def clip_up(e):
                dve.tensor_scalar(lc[:, :].rearrange("p (b n) -> p b n", b=2), ps[:, 2:4, :], -LIMIT, LIMIT, ALU.max, ALU.min).then_inc(gu_free, 2)
                dve.wait_ge(gu_free, (e + 1) * 2)
                dve.wait_ge(gm_done, e + 1)
                dve.scalar_tensor_tensor(lc[:, :], lc[:, :], 1.0, gm[:, :], ALU.add, ALU.mult).then_inc(lin_done, 1)

            def finish_act(e):
                dve.wait_ge(lin_done, e + 1)
                dve.wait_ge(sg_done, e + 1)
                dve.tensor_tensor(ac[:, :], lc[:, :], sg[:, :], ALU.mult).then_inc(ac_done, 1)

            def body(e):
                if e is None:
                    for m in range(DN):
                        lo_split(E, m)
                        if m == 1:
                            a_lo(E - 1)
                    return
                first = isinstance(e, int) and e == 0
                for n in range(EARLY if first else 0, GU if first else PER):
                    lo_split(e, n)
                    if n == BUFS - 1:
                        x_lo(0) if first else a_lo(e - 1)
                    if n == PER - 2:
                        clamp_gate(e)
                if first:
                    clamp_gate(0)
                clip_up(e)
                x_lo(e + 1)
                finish_act(e)

            iterations(dve, body)
            dve.wait_ge(y_out, 16 * E)
            many = dve.value_load(most[0:1, 0:1], min_val=0, max_val=SEQ)
            with dve.If(many > BLK):
                with dve.Fori(1, E * (NBLK - 1) + 1) as b:
                    dve.wait_ge(more_gu, b)
                    dve.tensor_scalar(gm[:, :].rearrange("p (b n) -> p b n", b=2), ps[:, 0:2, :], LIMIT, None, ALU.min).then_inc(more_act, 1)
                    dve.tensor_scalar(lc[:, :].rearrange("p (b n) -> p b n", b=2), ps[:, 2:4, :], -LIMIT, LIMIT, ALU.max, ALU.min).then_inc(more_lin, 1)
                    dve.wait_ge(more_act, 2 * b - 1)
                    dve.wait_ge(more_lin, 2 * b - 1)
                    dve.scalar_tensor_tensor(lc[:, :], lc[:, :], 1.0, gm[:, :], ALU.add, ALU.mult).then_inc(more_lin, 1)
                    dve.wait_ge(more_lin, 2 * b)
                    dve.wait_ge(more_sig, b)
                    dve.tensor_tensor(ac[:, :], lc[:, :], sg[:, :], ALU.mult).then_inc(more_act, 1)
            for t in range(NT):
                for k in range(TOPK):
                    dve.wait_ge(yg_in[t * TOPK + k], 16)
                    i_ = dve.scalar_tensor_tensor(x2[:, t, :], yg[:, t, k, :], gw[:, t, k:k + 1], x2[:, t, :], ALU.mult, ALU.add)
                    if k < TOPK - 1:
                        link(i_)
                i_.then_inc(summed, 1)

        def routing_pool(pool):
            count = [0]

            def after(ins):
                count[0] += 1
                ins.then_inc(pool_step, 1)
                pool.wait_ge(pool_step, count[0])

            after(pool.memset(pick[:, :], 1.0))
            pick3 = pick[:, :].rearrange("p (e n) -> p e n", n=P)
            for q in range(3):
                part = pick3[q * E:(q + 1) * E]
                i_ = pool.affine_select(out=part, in_=part, compare_op=ALU.is_equal, fill=0.0, base=0, pattern=[[-1, E], [0, P]],
                                        channel_multiplier=1)
                if q < 2:
                    after(i_)
            i_.then_inc(picks_ready, 1)
            pool.wait_ge(picks_ready, 1)
            pool.wait_ge(iota_read, 1)
            after(pool.memset(xg[:, :], 0.0))
            pool.wait_ge(hf_out, 16 * NT)
            pool.wait_ge(tok_ready, 1)


            def gather(column, into):
                after_now(pool.tensor_copy(now[:, 0:1], tok[:, bass.ds(column, 1)]))
                pool.indirect_dma_start(xg[:, :], None, hf_d[:, :], bass.IndirectOffsetOnAxis(ap=now[:, 0:1], axis=0),
                                        bounds_check=column + (SEQ - 1), oob_is_err=False).then_inc(into, 16)

            def scatter(column, into):
                after_now(pool.tensor_copy(now[:, 1:2], row[:, bass.ds(column, 1)]))
                pool.indirect_dma_start(y_d[:, :], bass.IndirectOffsetOnAxis(ap=now[:, 1:2], axis=0), yo[:, :], None,
                                        bounds_check=column + (SEQ * TOPK - 1), oob_is_err=False).then_inc(into, 16)

            def after_now(ins):
                ins.then_inc(pool_now, 1)
                pool.wait_ge(pool_now, turn[0])

            turn = [1]
            gather(0, xg_in)

            def body(e):
                if e is None:
                    turn[0] = 2 * E
                    pool.wait_ge(dn_free, E - 1)
                    pool.wait_ge(y_out, 16 * (E - 2))
                    scatter(E - 2, y_out)
                    pool.wait_ge(dn_free, E)
                    turn[0] = 2 * E + 1
                    pool.wait_ge(y_out, 16 * (E - 1))
                    scatter(E - 1, y_out)
                    return
                early = isinstance(e, int) and e < 2
                if not early:
                    turn[0] = 2 * e
                    pool.wait_ge(dn_free, e - 1)
                    if not (isinstance(e, int) and e == 2):
                        pool.wait_ge(y_out, (e - 2) * 16)
                    scatter(e - 2, y_out)
                    turn[0] = 2 * e + 1
                else:
                    turn[0] = e + 2
                pool.wait_ge(x_turned, e + 1)
                gather(e + 1, xg_in)

            iterations(pool, body)

            pool.wait_ge(y_out, 16 * E)
            pool.wait_ge(most_ready, 1)
            many = pool.value_load(most[0:1, 0:1], min_val=0, max_val=SEQ)
            with pool.If(many > BLK):
                with pool.Fori(E, E * NBLK) as b:
                    turn[0] = b * 2 + 2
                    pool.wait_ge(y_out, b * 16)
                    gather(b, more_x)
                    turn[0] = b * 2 + 3
                    pool.wait_ge(more_y, b - (E - 1))
                    scatter(b, y_out)

        block = ctx.enter_context(nc.Block())

        @block.sync
        def _(sp_):
            for n, (g, t) in enumerate(TILES):
                if n == 0:
                    for r in range(NT, NT + MT):
                        sp_.dma_start(xm[:, r, :], a["mem"][0][(r - NT) * P:(r - NT + 1) * P, :]).then_inc(xm_in[r], 16)
                if n == 1:
                    for r in range(NT):
                        sp_.dma_start(xm[:, r, :], a["x"][0][r * P:(r + 1) * P, :]).then_inc(xm_in[r], 16)
                s = n % SLOTS_MIX
                if n >= SLOTS_MIX:
                    sp_.wait_ge(w_lo, n - SLOTS_MIX + 1)
                sp_.dma_start(ring[:, s, :].rearrange("p (k n) -> p k n", k=4), weight_source(g, t)).then_inc(w_in[s], 16)
            if not stop_after_mixer:
                experts_sync(sp_)

        @block.scalar
        def _(act):
            nc.scalar.preload_act_table_set("natural_log_exp_and_others")
            steps_seen = 0
            for step in STEPS:
                kind, x = step[0], step[1:]
                if kind == "rms":
                    which, = x
                    for n, r in enumerate(TILES_OF[which]):
                        act.wait_ge(xm_in[r], 16)
                        if BEFORE[which] + n:
                            act.wait_ge(squared, BEFORE[which] + n)
                        act.activation(sqd[:, :], xm[:, r, :], ACT.Square, accum_out=ssx[:, r:r + 1]).then_inc(squared, 1)
                    rows_ = slice(TILES_OF[which][0], TILES_OF[which][-1] + 1)
                    act.wait_ge(mean_ready, 1 + (which == "x"))
                    act.activation(rx[:, rows_], mx_[:, rows_], ACT.Ln).then_inc(act_step, 1)
                    steps_seen += 1
                    act.wait_ge(act_step, steps_seen)
                    act.activation(rx[:, rows_], rx[:, rows_], ACT.Exp, scale=-0.5).then_inc(root_ready, 1)
                elif kind == "turn":
                    which, = x
                    gain, hi, _lo, n = HALF[which]
                    act.wait_ge(gain_in, 16 * len(first_loads))
                    for k in range(KD):
                        act.wait_ge(turned, KD * (which == "x") + k + 1)
                        act.activation(hi[:, k, :], ps[:, turn_bank(which, k), 0:n], ACT.Copy, scale=gain[:, k:k + 1]).then_inc(h_hi, 1)
                elif kind == "split":
                    n, = x
                    s = n % SLOTS_MIX
                    act.wait_ge(w_in[s], 16 * (n // SLOTS_MIX + 1))
                    if n >= 2:
                        act.wait_ge(unit_done, USED[n - 2])
                    act.activation(split(n)[0], ring[:, s, :], ACT.Copy).then_inc(w_hi, 1)
                elif kind == "save" and BY_ACT(x[0]):
                    g, c = x
                    act.wait_ge(unit_done, SUMMED[x])
                    if g in NORMED:
                        y = NORMS[x] - 1
                        if y >= 2:
                            act.wait_ge(ssum_done, y - 1)
                        act.activation(nsq[:, y % 2, 0:GROUPS[g][1]], chunk(g, c), ACT.Square).then_inc(nsq_ready, 1)
                        act.activation(normed_chunk(g, c), chunk(g, c), ACT.Copy).then_inc(saved_act, 1)
                    elif g in LATE:
                        place, had = LATE[g]
                        act.wait_ge(saved_dve, SAVED_DVE[had, c])
                        act.activation(gate[:, place, c, :], chunk(g, c), ACT.Sigmoid).then_inc(saved_act, 1)
                    else:
                        dst = {"mv": vm, "v": v, "cc": cu}[g][:, c, :] if g in ("mv", "v", "cc") else gate[:, EARLY_GATES.index(g), c, :]
                        act.activation(dst, chunk(g, c), ACT.Copy).then_inc(saved_act, 1)
                elif kind == "save" and x[0][:2] == "b2":
                    g, c = x
                    d = 4 * int(g[2]) + c
                    act.wait_ge(unit_done, SUMMED["b11", 3])
                    act.wait_ge(acc_done, d + 1)
                    act.activation(gh[:, d, :], acc[:, d, :], ACT.Copy).then_inc(gh_done, 1)
                elif kind == "norm":
                    g, c = x
                    y = NORMS[x] - 1
                    n = GROUPS[g][1]
                    act.wait_ge(nm_ready, y + 1)
                    act.activation(ny[:, y % 2, 0:n], nm_[:, y % 2, 0:n], ACT.Ln).then_inc(act_step, 1)
                    steps_seen += 1
                    act.wait_ge(act_step, steps_seen)
                    act.activation(ny[:, y % 2, 0:n], ny[:, y % 2, 0:n], ACT.Exp, scale=-0.5).then_inc(ny_ready, 1)
                elif kind == "msoft":
                    h, = x
                    act.wait_ge(mneg_ready, h + 1)
                    if h:
                        act.wait_ge(mt_done, h)
                    for t in range(NT):
                        e_ = act.activation(pm[:, t, :], ps[:, 4 + t // 2, (t % 2) * MEM:(t % 2 + 1) * MEM], ACT.Exp,
                                            bias=mneg_[:, t:t + 1], scale=SCALE_M, accum_out=msum[:, t:t + 1])
                    e_.then_inc(mexp_done, 1)
                elif kind == "mturn":
                    h, = x
                    act.wait_ge(mt_done, h + 1)
                    if h:
                        act.wait_ge(mo_done, h)
                    act.activation(pT[:, 0, :], ps[:, 6, :], ACT.Copy).then_inc(mt_act, 1)
                elif kind == "soft":
                    h, = x
                    act.wait_ge(z_done, h + 1)
                    if h:
                        act.wait_ge(sp_done, 2 * h)
                    for b, (lo, hi) in (((2, 3), (OFF[2], PACKED)), ((0, 1), (0, OFF[2]))):
                        for i in b:
                            e_ = act.activation(we[:, OFF[i]:OFF[i] + WIDTH[i]], ps[:, 4 + i, P * i:SEQ], ACT.Abs)
                        e_.then_inc(act_step, 1)
                        steps_seen += 1
                        act.wait_ge(act_step, steps_seen)
                        act.activation(we[:, lo:hi], we[:, lo:hi], ACT.Exp, scale=-1.0).then_inc(act_step, 1)
                        steps_seen += 1
                        act.wait_ge(act_step, steps_seen)
                        act.activation(we[:, lo:hi], we[:, lo:hi], ACT.Ln, bias=1.0).then_inc(log_done, 1)
                elif kind == "between":
                    h, = x
                    if h:
                        act.wait_ge(av_done, h)
                    for n, i in enumerate(reversed(range(NT))):
                        act.wait_ge(c_done, NT * h + n + 1)
                        act.activation(w[:, OFF[i]:OFF[i] + WIDTH[i]], ps[:, 4 + i, P * i:SEQ], ACT.Exp).then_inc(w_done, 1)
                elif kind == "ochunk":
                    c, = x
                    act.wait_ge(o_saved, 2 * c + 2)
                    act.activation(oh[0][:, c, :], osb[:, c, :], ACT.Copy).then_inc(oh_done, 1)
                elif kind == "osplit":
                    i, = x
                    act.wait_ge(saved_dve, SAVED_DVE["cb", 3])
                    act.activation(oh[i][:, :, :], (osb, oc, om)[i][:, :, :], ACT.Copy).then_inc(oh_done, 1)
                elif kind == "sig":
                    i, = x
                    act.wait_ge(saved_act, SAVED_ACT[EARLY_GATES[i], 3])
                    act.activation(gate[:, i], gate[:, i], ACT.Sigmoid).then_inc(sig_done, 1)
                elif kind == "square":
                    t, = x
                    if t == 0:
                        act.wait_ge(gl_done, KD)
                        nc.scalar.preload_act_table_set("natural_log_exp_and_others")
                    else:
                        act.wait_ge(squared2, t)
                    act.wait_ge(saved_dve, SAVED_DVE["o1", t])
                    act.activation(sq2[:, :], x2[:, t, :], ACT.Square, accum_out=ss2[:, t:t + 1]).then_inc(squared2, 1)
                elif kind == "root":
                    n, = x
                    pair = slice(2 * n, 2 * n + 2)
                    act.wait_ge(m2_ready, n + 1)
                    act.activation(r2[:, pair], m2[:, pair], ACT.Ln).then_inc(act_step, 1)
                    steps_seen += 1
                    act.wait_ge(act_step, steps_seen)
                    act.activation(r2[:, pair], r2[:, pair], ACT.Exp, scale=-0.5).then_inc(r2_ready, 1)
            if not stop_after_mixer:
                routing_act(act)

        @block.tensor
        def _(pe):
            pe.wait_ge(made, MADE)
            pe.wait_ge(made_dve, 1)
            for step in STEPS:
                kind, x = step[0], step[1:]
                if kind == "turn":
                    which, = x
                    pe.wait_ge(scaled, BEFORE[which] + len(TILES_OF[which]))
                    for k in range(KD):
                        if which == "x" and k >= 4:
                            pe.wait_ge(h_lo, KD + k - 3)
                        for n, r in enumerate(TILES_OF[which]):
                            mm = pe.transpose(ps[:, turn_bank(which, k), n * P:(n + 1) * P], xm[:, r, k * P:(k + 1) * P], ident[:, :])
                        mm.then_inc(turned, 1)
                elif kind == "unit":
                    g, t, c = x
                    n = NUMBER[g, t]
                    if (t, c) == (0, 0) and g in ("mk", "q"):
                        pe.wait_ge(h_lo, KD * (1 + (g == "q")))
                    if c == 0:
                        pe.wait_ge(w_lo, n + 1)
                    if t == 0 and FREED_BY[g, c]:
                        by = FREED_BY[g, c]
                        if BY_ACT(by[0]):
                            pe.wait_ge(saved_act, SAVED_ACT[by])
                        else:
                            pe.wait_ge(saved_dve, SAVED_DVE[by])
                    if g[0] == "b":
                        pe.wait_ge(osplit_done, SBH // 2 + int(g[1]))
                    if g[0] == "o":
                        pe.wait_ge(gl_done, 4 * t + 4)
                    hi, lo = operands(g)
                    whi, wlo = (z_.rearrange("p (k n) -> p k n", k=4) for z_ in split(n))
                    last = GROUPS[g][0] - 1
                    for k in range(4):
                        for z_, (av_, wv_) in enumerate(((hi, whi), (hi, wlo), (lo, whi))):
                            if g in TOKEN_MAJOR:
                                lhs, rhs = av_[:, 4 * t + k, c * P:(c + 1) * P], wv_[:, k, :]
                            else:
                                lhs, rhs = wv_[:, k, c * P:(c + 1) * P], av_[:, 4 * t + k, :]
                            mm = pe.matmul(chunk(g, c), lhs, rhs, start=(t == 0 and k == 0 and z_ == 0),
                                           stop=(t == last and k == 3 and z_ == 2))
                    mm.then_inc(unit_done, 1)
                elif kind == "ssum":
                    y = NORMS[x] - 1
                    n = GROUPS[x[0]][1]
                    if y == 0:
                        pe.wait_ge(h_lo, 2 * KD)
                    pe.wait_ge(nsq_ready, y + 1)
                    if y >= 4:
                        pe.wait_ge(nm_ready, y - 3)
                    pe.matmul(ps[:, 4 + y % 4, 0:n], (halves if x[0] in "qk" else ones)[:, :], nsq[:, y % 2, 0:n],
                              start=True, stop=True).then_inc(ssum_done, 1)
                elif kind == "mscore":
                    h, = x
                    if h == 0:
                        pe.wait_ge(normed, len(NORMS))
                    else:
                        pe.wait_ge(om_saved, h)
                    for t in range(NT):
                        mm = pe.matmul(ps[:, 4 + t // 2, (t % 2) * MEM:(t % 2 + 1) * MEM], qm[:, h, t * P:(t + 1) * P],
                                       km[:, h, :], start=True, stop=True)
                    mm.then_inc(ms_done, 1)
                elif kind == "mturn":
                    h, = x
                    pe.wait_ge(mprob_ready, h + 1)
                    if h:
                        pe.wait_ge(mt_act, h)
                        pe.wait_ge(mt_dve, h)
                    for m in range(MT):
                        for t in range(NT):
                            mm = pe.transpose(ps[:, 6 + m, t * P:(t + 1) * P], pm[:, t, m * P:(m + 1) * P], ident[:, :])
                    mm.then_inc(mt_done, 1)
                elif kind == "mout":
                    h, = x
                    pe.wait_ge(mt_act, h + 1)
                    pe.wait_ge(mt_dve, h + 1)
                    pe.wait_ge(saved_act, SAVED_ACT["mv", MT - 1])
                    for m in range(MT):
                        mm = pe.matmul(ps[:, 4, :], vm[:, m, h * P:(h + 1) * P], pT[:, m, :], start=(m == 0), stop=(m == MT - 1))
                    mm.then_inc(mo_done, 1)
                elif kind == "z":
                    h, = x
                    lo = DH * (h % 2)
                    if h == 0:
                        pe.wait_ge(om_saved, MH)
                    else:
                        pe.wait_ge(o_saved, h)
                    for i in range(NT):
                        pe.matmul(ps[:, 4 + i, P * i:SEQ], kT[lo:lo + DH, h // 2, P * i:P * (i + 1)],
                                  qT[lo:lo + DH, h // 2, P * i:SEQ], start=True, stop=True)
                        mm = pe.matmul(ps[:, 4 + i, P * i:P * (i + 1)], identb[:, :], maskb[:, :], start=False, stop=True,
                                       skip_group_check=True)
                    mm.then_inc(z_done, 1)
                elif kind == "between":
                    h, = x
                    for n, pair in enumerate(((3, 2), (1, 0))):
                        for part, ready in ((sph, sph_done), (spl, spl_done)):
                            pe.wait_ge(ready, 2 * h + n + 1)
                            for i in pair:
                                for j in range(i, NT):
                                    mm = pe.matmul(ps[:, 4 + i, P * j:SEQ], (down if j == i else minus)[:, :],
                                                   part[:, OFF[j]:OFF[j] + WIDTH[j]], start=False, stop=True,
                                                   skip_group_check=True)
                                if part is spl:
                                    mm.then_inc(c_done, 1)
                elif kind == "av":
                    h, = x
                    lo = DH * (h % 2)
                    pe.wait_ge(w_done, NT * (h + 1))
                    pe.wait_ge(saved_act, SAVED_ACT["v", NT - 1])
                    for i in range(NT):
                        mm = pe.matmul(ps[lo:lo + DH, 4, P * i:SEQ], v[:, i, DH * h:DH * (h + 1)],
                                       w[:, OFF[i]:OFF[i] + WIDTH[i]], start=(i == 0), stop=True,
                                       skip_group_check=True)
                    mm.then_inc(av_done, 1)
            if not stop_after_mixer:
                routing_pe(pe)

        @block.vector
        def _(dve):
            chain = [0]

            def link(ins):
                chain[0] += 1
                ins.then_inc(dve_step, 1)
                dve.wait_ge(dve_step, chain[0])

            dve.wait_ge(made, MADE)
            dve.memset(minus[:, :].bitcast(F32), -1.0)
            dve.tensor_copy(down[:, :], downf[:, :]).then_inc(made_dve, 1)

            def newton(r, m, t):
                link(dve.scalar_tensor_tensor(t, r, -0.5, r, ALU.mult, ALU.mult))
                link(dve.tensor_tensor(t, t, m, ALU.mult))
                link(dve.scalar_tensor_tensor(r, t, 1.5, r, ALU.add, ALU.mult))

            for step in STEPS:
                kind, x = step[0], step[1:]
                if kind == "rms":
                    which, = x
                    rows_ = slice(TILES_OF[which][0], TILES_OF[which][-1] + 1)
                    half = 1 + (which == "x")
                    dve.wait_ge(squared, BEFORE[which] + len(TILES_OF[which]))
                    dve.tensor_scalar(mx_[:, rows_], ssx[:, rows_], 1.0 / D, EPS, ALU.mult, ALU.add).then_inc(mean_ready, 1)
                    dve.wait_ge(mean_ready, half)
                    dve.wait_ge(root_ready, half)
                    newton(rx[:, rows_], mx_[:, rows_], tx[:, rows_])
                    for r in TILES_OF[which]:
                        dve.tensor_scalar(xm[:, r, :], xm[:, r, :], rx[:, r:r + 1], None, ALU.mult).then_inc(scaled, 1)
                elif kind == "turn":
                    which, = x
                    gain, hi, lo, n = HALF[which]
                    for k in range(KD):
                        dve.wait_ge(h_hi, KD * (which == "x") + k + 1)
                        dve.scalar_tensor_tensor(lo[:, k, :], ps[:, turn_bank(which, k), 0:n], gain[:, k:k + 1],
                                                 hi[:, k, :].bitcast(F32), ALU.mult, ALU.subtract).then_inc(h_lo, 1)
                    if which == "x":
                        dve.wait_ge(small_in, 16 * len(small_loads))
                        link(dve.tensor_scalar(qg, qg, DH ** -0.5, None, ALU.mult))
                elif kind == "split":
                    n, = x
                    dve.wait_ge(w_hi, n + 1)
                    hi, lo = split(n)
                    dve.tensor_tensor(lo, ring[:, n % SLOTS_MIX, :], hi.bitcast(F32), ALU.subtract).then_inc(w_lo, 1)
                elif kind == "save" and not BY_ACT(x[0]):
                    g, c = x
                    dve.wait_ge(unit_done, SUMMED[x])
                    if g == "cx":
                        dve.wait_ge(saved_act, SAVED_ACT["cc", c])
                        dve.tensor_tensor(cu[:, c, :], chunk(g, c), cu[:, c, :], ALU.mult).then_inc(saved_dve, 1)
                        dve.wait_ge(saved_dve, SAVED_DVE[x])
                        link(dve.tensor_scalar(oc[:, c, :], cu[:, c, :], taps[:, 8 + c:9 + c], None, ALU.mult))
                        link(dve.scalar_tensor_tensor(oc[:, c, 1:SEQ], cu[:, c, 0:SEQ - 1], taps[:, 4 + c:5 + c],
                                                      oc[:, c, 1:SEQ], ALU.mult, ALU.add))
                        link(dve.scalar_tensor_tensor(oc[:, c, 2:SEQ], cu[:, c, 0:SEQ - 2], taps[:, c:c + 1],
                                                      oc[:, c, 2:SEQ], ALU.mult, ALU.add))
                    elif g == "cb":
                        dve.tensor_tensor(oc[:, c, :], chunk(g, c), oc[:, c, :], ALU.mult).then_inc(saved_dve, 1)
                    elif g[0] == "b":
                        i, d = int(g[1]), 4 * int(g[2]) + c
                        late = [q for q in LATE if PLACE[g] == LATE[q][0] and q[1:] == g[1:]]
                        if late:
                            dve.wait_ge(saved_act, SAVED_ACT[late[0], c])
                        else:
                            dve.wait_ge(sig_done, EARLY_GATES.index("g" + g[1:]) + 1)
                        if i == 0:
                            dve.tensor_tensor(acc[:, d, :], chunk(g, c), gate[:, PLACE[g], c, :], ALU.mult).then_inc(saved_dve, 1)
                        else:
                            dve.tensor_tensor(tmp[:, c % 2, :], chunk(g, c), gate[:, PLACE[g], c, :], ALU.mult).then_inc(saved_dve, 1)
                            dve.wait_ge(saved_dve, SAVED_DVE[x])
                            add = dve.tensor_tensor(acc[:, d, :], acc[:, d, :], tmp[:, c % 2, :], ALU.add)
                            if i == 1:
                                link(add)
                            else:
                                add.then_inc(acc_done, 1)
                                dve.wait_ge(gh_done, d + 1)
                                dve.tensor_tensor(gl[:, d, :], acc[:, d, :], gh[:, d, :].bitcast(F32), ALU.subtract).then_inc(gl_done, 1)
                    else:
                        cols_ = slice(int(g[1]) * G, (int(g[1]) + 1) * G)
                        dve.wait_ge(xr_in, 16)
                        dve.tensor_tensor(x2[:, c, cols_], chunk(g, c), xr[:, c, cols_], ALU.add).then_inc(saved_dve, 1)
                elif kind == "norm":
                    g, c = x
                    y = NORMS[x] - 1
                    n = GROUPS[g][1]
                    m, r, t = (z_[:, y % 2, 0:n] for z_ in (nm_, ny, nt_))
                    dve.wait_ge(ssum_done, y + 1)
                    dve.tensor_scalar(m, ps[:, 4 + y % 4, 0:n], 1.0 / (DH if g in "qk" else P), EPS, ALU.mult, ALU.add).then_inc(nm_ready, 1)
                    dve.wait_ge(nm_ready, y + 1)
                    dve.wait_ge(ny_ready, y + 1)
                    newton(r, m, t)
                    dve.wait_ge(saved_act, SAVED_ACT[x])
                    dve.scalar_tensor_tensor(normed_chunk(g, c), normed_chunk(g, c), GAIN[g], r, ALU.mult, ALU.mult).then_inc(normed, 1)
                elif kind == "msoft":
                    h, = x
                    dve.wait_ge(ms_done, h + 1)
                    link(dve.tensor_reduce(mmax, ps[:, 4:6, :].rearrange("p b (t m) -> p (b t) m", m=MEM), AX.X, ALU.max))
                    dve.tensor_scalar(mneg_, mmax, -SCALE_M, None, ALU.mult).then_inc(mneg_ready, 1)
                    dve.wait_ge(mexp_done, h + 1)
                    link(dve.reciprocal(mrec, msum))
                    for t in range(NT):
                        e_ = dve.tensor_scalar(pm[:, t, :], pm[:, t, :], mrec[:, t:t + 1], None, ALU.mult)
                    e_.then_inc(mprob_ready, 1)
                elif kind == "mturn":
                    h, = x
                    dve.wait_ge(mt_done, h + 1)
                    if h:
                        dve.wait_ge(mo_done, h)
                    dve.tensor_copy(pT[:, 1, :], ps[:, 7, :]).then_inc(mt_dve, 1)
                elif kind == "mout":
                    h, = x
                    dve.wait_ge(mo_done, h + 1)
                    dve.tensor_copy(om[:, h, :], ps[:, 4, :]).then_inc(om_saved, 1)
                elif kind == "soft":
                    h, = x
                    for n, b in enumerate(((2, 3), (0, 1))):
                        dve.wait_ge(log_done, 2 * h + n + 1)
                        for i in b:
                            e_ = dve.scalar_tensor_tensor(sp[:, OFF[i]:OFF[i] + WIDTH[i]], ps[:, 4 + i, P * i:SEQ], 0.0,
                                                          we[:, OFF[i]:OFF[i] + WIDTH[i]], ALU.max, ALU.add)
                        e_.then_inc(sp_done, 1)
                        dve.wait_ge(sp_done, 2 * h + n + 1)
                        lo, hi = OFF[b[0]], OFF[b[1]] + WIDTH[b[1]]
                        if h:
                            dve.wait_ge(c_done, NT * h)
                        dve.tensor_copy(sph[:, lo:hi], sp[:, lo:hi]).then_inc(sph_done, 1)
                        dve.wait_ge(sph_done, 2 * h + n + 1)
                        dve.tensor_tensor(spl[:, lo:hi], sp[:, lo:hi], sph[:, lo:hi].bitcast(F32), ALU.subtract).then_inc(spl_done, 1)
                elif kind == "av":
                    h, = x
                    lo = DH * (h % 2)
                    dve.wait_ge(av_done, h + 1)
                    dve.tensor_copy(osb[lo:lo + DH, h // 2, :], ps[lo:lo + DH, 4, :]).then_inc(o_saved, 1)
                elif kind == "ochunk":
                    c, = x
                    dve.wait_ge(oh_done, c + 1)
                    dve.tensor_tensor(ol[0][:, c, :], osb[:, c, :], oh[0][:, c, :].bitcast(F32), ALU.subtract).then_inc(osplit_done, 1)
                elif kind == "osplit":
                    i, = x
                    dve.wait_ge(oh_done, SBH // 2 + i)
                    dve.tensor_tensor(ol[i][:, :, :], (osb, oc, om)[i][:, :, :], oh[i][:, :, :].bitcast(F32), ALU.subtract).then_inc(osplit_done, 1)
                elif kind == "bias":
                    c, = x
                    dve.wait_ge(braw_in, 16 * 6)
                    raw, parts = braw[:, c * FF:(c + 1) * FF], ebias[:, c * FF:(c + 1) * FF]
                    part = [slice(q * E, (q + 1) * E) for q in range(3)]
                    link(dve.tensor_copy(parts, raw))
                    for q in (1, 2):
                        for u in range(q, 3):
                            i_ = dve.tensor_tensor(raw[part[u]], raw[part[u]], parts[part[u]], ALU.subtract)
                        link(i_)
                        for u in range(q, 3):
                            i_ = dve.tensor_copy(parts[part[u]], raw[part[u]])
                        if q == 1:
                            link(i_)
                    i_.then_inc(ebias_ready, 1)
                elif kind == "root":
                    n, = x
                    pair = slice(2 * n, 2 * n + 2)
                    dve.wait_ge(squared2, 2 * n + 2)
                    dve.tensor_scalar(m2[:, pair], ss2[:, pair], 1.0 / D, EPS, ALU.mult, ALU.add).then_inc(m2_ready, 1)
                    dve.wait_ge(m2_ready, n + 1)
                    dve.wait_ge(r2_ready, n + 1)
                    newton(r2[:, pair], m2[:, pair], t2[:, pair])
                elif kind == "scale":
                    n, = x
                    for t in (2 * n, 2 * n + 1):
                        dve.scalar_tensor_tensor(hf[:, t, :], x2[:, t, :], r2[:, t:t + 1], gbc[:, :], ALU.mult, ALU.mult).then_inc(hf_done, 1)
            if not stop_after_mixer:
                routing_dve(dve, link)

        @block.gpsimd
        def _(pool):
            for dst, src in first_loads:
                pool.dma_start(dst, src).then_inc(gain_in, 16)
            count = [0]

            def after(ins):
                count[0] += 1
                ins.then_inc(made, 1)
                pool.wait_ge(made, count[0])

            for m, value in ((ident, 0.0), (identb, 0.0), (ones, 1.0), (onesb, 1.0), (halves, 0.0), (downf, -1.0),
                             (maskb, MASKED), (before, 1.0)):
                after(pool.memset(m[:, :], value))
            after(pool.memset(halves[0:DH, 0:DH], 1.0))
            after(pool.memset(halves[DH:P, DH:P], 1.0))
            for m, op, fill, step_, per in ((ident, ALU.not_equal, 1.0, -1, 1), (identb, ALU.not_equal, 1.0, -1, 1),
                                            (downf, ALU.is_ge, 0.0, -1, 1), (maskb, ALU.is_ge, 0.0, -1, 1),
                                            (before, ALU.is_gt, 0.0, 1, -1)):
                after(pool.affine_select(out=m[:, :], in_=m[:, :], compare_op=op, fill=fill, base=0, pattern=[[step_, P]],
                                         channel_multiplier=per))
            for dst, src in small_loads:
                pool.dma_start(dst, src).then_inc(small_in, 16)
            pool.wait_ge(unit_done, UNIT["g21", 1, 3])
            pool.dma_start(xr[:, :, :], a["x"][0].rearrange("(t p) d -> p t d", p=P)).then_inc(xr_in, 16)
            pool.wait_ge(gl_done, KD)
            for q in range(3):
                pool.dma_start(braw[q * E:(q + 1) * E, 0:2 * FF], a["b_gate_up"][0]).then_inc(braw_in, 16)
                pool.dma_start(braw[q * E:(q + 1) * E, 2 * FF:3 * FF], a["b_down"][0]).then_inc(braw_in, 16)
            pool.dma_start(wr[:, :, :], a["w_router"][0].rearrange("(k p) e -> p k e", p=P)).then_inc(wr_in, 16)
            after(pool.iota(iotai[:, :], pattern=[[1, COLS]], base=0, channel_multiplier=0))
            pool.iota(rows[:, :], pattern=[[TOPK * P, NT], [1, TOPK]], base=0, channel_multiplier=TOPK).then_inc(rmade, 1)
            pool.wait_ge(rmade, 1)
            pool.wait_ge(braw_in, 16 * 6)
            raw, parts = braw[:, 2 * FF:3 * FF], ebias[:, 2 * FF:3 * FF]
            for q in range(3):
                mine = slice(q * E, (q + 1) * E)
                for _ in range(q):
                    after(pool.tensor_copy(parts[mine], raw[mine]))
                    after(pool.tensor_tensor(raw[mine], raw[mine], parts[mine], ALU.subtract))
                i_ = pool.tensor_copy(parts[mine], raw[mine])
                if q < 2:
                    after(i_)
            i_.then_inc(ebias_ready, 1)
            pool.wait_ge(ebias_ready, 3)
            if stop_after_mixer:
                pool.wait_ge(saved_dve, SAVED_DVE["o1", NT - 1])
                pool.dma_start(out[0].rearrange("(t p) d -> p t d", p=P), x2[:, :, :]).then_inc(out_done, 16)
                pool.wait_ge(out_done, 16)
            else:
                routing_pool(pool)


_INS = ["x", "mem", "mix_norm_g", "w_in", "sb_q_norm_g", "sb_k_norm_g", "conv_w", "mem_norm_g", "w_mem_kv",
        "mem_q_norm_g", "mem_k_norm_g", "w_br_sb", "w_br_conv", "w_br_mem", "w_o", "ffn_norm_g", "w_router", "b_router",
        "w_gate_up", "b_gate_up", "w_down", "b_down"]
_OUTS = [((1, 512, 1024), "float32")]


def kernel(**inputs):
    import numpy as _np
    import concourse.bacc as _bacc
    from concourse import mybir as _mybir
    from concourse.bass_utils import run_bass_kernel_spmd as _run

    nc = _bacc.Bacc("TRN2", target_bir_lowering=False, num_devices=1)
    arrays, aps = {}, {}
    for name in _INS:
        x = _np.ascontiguousarray(inputs[name])
        arrays[f"in_{name}_dram"] = x
        aps[name] = nc.dram_tensor(f"in_{name}_dram", x.shape, _mybir.dt.from_np(x.dtype), kind="ExternalInput").ap()
    shape, dtype = _OUTS[0]
    out = nc.dram_tensor("out_0_dram", shape, _mybir.dt.from_np(_np.dtype(dtype)), kind="ExternalOutput").ap()
    build(nc, aps, out)
    r = _run(nc, [arrays], core_ids=[0])
    return r.results[0]["out_0_dram"]
```
